# Optimizing a Trainium2 kernel written in Bass

```python
import jax, jax.numpy as jnp
from jax import lax
import numpy as np

D_MODEL = 1024
BATCH = 1
SEQ = 2048
DEPTH = 1
DEC_BATCH = 1
DEC_SEQ = 32
PAST_LEN = 2048

CHUNK = 64
POOL_WINDOWS = (2, 4, 8, 16)
N_POOL_GROUPS = 4
POOL_GROUP_DIM = 128
POOL_WIDTH = N_POOL_GROUPS * POOL_GROUP_DIM
POOL_OUT_GROUP = D_MODEL // N_POOL_GROUPS
POOL_BUF = max(POOL_WINDOWS) - 1
N_HEADS = 8
N_KV_HEADS = 2
HEAD_DIM = 64
Q_GROUP = N_HEADS // N_KV_HEADS
ATTN_WIDTH = N_HEADS * HEAD_DIM
KV_WIDTH = N_KV_HEADS * HEAD_DIM
WINDOW = 128
WINDOW_CHUNKS = WINDOW // CHUNK
ROPE_DIM = HEAD_DIM // 4
ROPE_THETA = 500000.0
D_FF = 4 * D_MODEL
RMS_EPS = 1e-6
IN_WIDTH = POOL_WIDTH + ATTN_WIDTH + 2 * KV_WIDTH + 2 * D_MODEL

kernel_name = "hybrid_pool_swa_sink_streaming_step"

def _rmsnorm(x, g):
    xf = x.astype(jnp.float32)
    y = xf * lax.rsqrt(jnp.mean(xf * xf, axis=-1, keepdims=True) + RMS_EPS)
    return (y * g.astype(jnp.float32)).astype(x.dtype)

def _rope(x, pos):
    inv = ROPE_THETA ** (-jnp.arange(0, ROPE_DIM, 2, dtype=jnp.float32) / ROPE_DIM)
    ang = pos.astype(jnp.float32)[:, None] * inv[None, :]
    cos = jnp.cos(ang)[:, None, :]
    sin = jnp.sin(ang)[:, None, :]
    xf = x.astype(jnp.float32)
    x1 = xf[..., : ROPE_DIM // 2]
    x2 = xf[..., ROPE_DIM // 2: ROPE_DIM]
    out = jnp.concatenate([x1 * cos - x2 * sin, x2 * cos + x1 * sin, xf[..., ROPE_DIM:]], axis=-1)
    return out.astype(x.dtype)

def _split_in(z):
    o1 = POOL_WIDTH
    o2 = o1 + ATTN_WIDTH
    o3 = o2 + KV_WIDTH
    o4 = o3 + KV_WIDTH
    o5 = o4 + D_MODEL
    return z[..., :o1], z[..., o1:o2], z[..., o2:o3], z[..., o3:o4], z[..., o4:o5], z[..., o5:]

def _pool_mix(xx, pos, w_pool, pool_scale):
    B, L, C = xx.shape
    T = pos.shape[0]
    xf = xx.astype(jnp.float32)
    cs = jnp.concatenate([jnp.zeros((B, 1, C), jnp.float32), jnp.cumsum(xf, axis=1)], axis=1)
    end = cs[:, POOL_BUF + 1:]
    x_tok = xf[:, POOL_BUF:]
    outs = []
    for g, w in enumerate(POOL_WINDOWS):
        sl = slice(g * POOL_GROUP_DIM, (g + 1) * POOL_GROUP_DIM)
        start = cs[:, POOL_BUF + 1 - w: POOL_BUF + 1 - w + T, sl]
        cnt = jnp.minimum(pos + 1, w).astype(jnp.float32)[None, :, None]
        outs.append((end[..., sl] - start) / cnt - x_tok[..., sl])
    p = jnp.stack(outs, axis=2).astype(w_pool.dtype)
    y = jnp.einsum('btgc,gcd->btgd', p, w_pool).reshape(B, T, D_MODEL)
    return y * pool_scale

def _win_mask(qp, kp):
    qc = qp // CHUNK
    kc = kp // CHUNK
    return (kp >= 0) & (kc <= qc) & (qc - kc < WINDOW_CHUNKS)

def _sink_attention(q, k, v, mask, sinks):
    s = jnp.einsum('bnqhgd,bnkhd->bnhgqk', q, k).astype(jnp.float32) * (HEAD_DIM ** -0.5)
    s = jnp.where(mask[None, :, None, None], s, -jnp.inf)
    sink = jnp.broadcast_to(sinks.astype(jnp.float32).reshape(N_KV_HEADS, Q_GROUP)[None, None, :, :, None, None],
                            s.shape[:-1] + (1,))
    p = jax.nn.softmax(jnp.concatenate([s, sink], axis=-1), axis=-1)[..., :-1]
    return jnp.einsum('bnhgqk,bnkhd->bnqhgd', p.astype(v.dtype), v)

def _banded_attention(q, k, v, sinks):
    B, T = q.shape[:2]
    nC = T // CHUNK
    qb = q.reshape(B, nC, CHUNK, N_KV_HEADS, Q_GROUP, HEAD_DIM)
    pad = jnp.zeros((B, WINDOW_CHUNKS - 1, CHUNK, N_KV_HEADS, HEAD_DIM), k.dtype)
    kb = jnp.concatenate([pad, k.reshape(B, nC, CHUNK, N_KV_HEADS, HEAD_DIM)], axis=1)
    vb = jnp.concatenate([pad, v.reshape(B, nC, CHUNK, N_KV_HEADS, HEAD_DIM)], axis=1)
    kwin = jnp.concatenate([kb[:, i:i + nC] for i in range(WINDOW_CHUNKS)], axis=2)
    vwin = jnp.concatenate([vb[:, i:i + nC] for i in range(WINDOW_CHUNKS)], axis=2)
    blk = jnp.arange(nC)[:, None]
    qpos = blk * CHUNK + jnp.arange(CHUNK)[None, :]
    kpos = (blk - (WINDOW_CHUNKS - 1)) * CHUNK + jnp.arange(WINDOW_CHUNKS * CHUNK)[None, :]
    mask = _win_mask(qpos[:, :, None], kpos[:, None, :])
    o = _sink_attention(qb, kwin, vwin, mask, sinks)
    return o.reshape(B, T, ATTN_WIDTH)

def _merge(pool_out, attn, gp, ga, w_attn_up, w_out):
    attn_out = attn @ w_attn_up
    merged = jax.nn.sigmoid(gp) * pool_out + jax.nn.sigmoid(ga) * attn_out
    return merged @ w_out

def _mlp(x, w_up, w_down):
    return jnp.square(jax.nn.relu(x @ w_up)) @ w_down

def setup_inputs(seed: int = 0) -> dict:
    key = jax.random.key(seed)
    ks = jax.random.split(key, 20)
    f32 = jnp.float32
    kv_buf = min(WINDOW, PAST_LEN)
    n = lambda k, s, sc: jax.random.normal(k, s, f32) * sc
    return {
        "x_prompt": n(ks[0], (BATCH, SEQ, D_MODEL), 1.0),
        "x_sample": n(ks[1], (DEC_BATCH, DEC_SEQ, D_MODEL), 1.0),
        "cache_k": n(ks[2], (DEPTH, DEC_BATCH, kv_buf, N_KV_HEADS, HEAD_DIM), 1.0),
        "cache_v": n(ks[3], (DEPTH, DEC_BATCH, kv_buf, N_KV_HEADS, HEAD_DIM), 1.0),
        "state_pool": n(ks[4], (DEPTH, DEC_BATCH, POOL_BUF, POOL_WIDTH), 1.0),
        "norm_mix": 1.0 + n(ks[5], (DEPTH, D_MODEL), 0.02),
        "w_in": n(ks[6], (DEPTH, D_MODEL, IN_WIDTH), D_MODEL ** -0.5),
        "sinks": n(ks[7], (DEPTH, N_HEADS), 0.5),
        "w_pool": n(ks[8], (DEPTH, N_POOL_GROUPS, POOL_GROUP_DIM, POOL_OUT_GROUP), POOL_GROUP_DIM ** -0.5),
        "pool_scale": 1.0 + n(ks[9], (DEPTH, D_MODEL), 0.02),
        "w_attn_up": n(ks[10], (DEPTH, ATTN_WIDTH, D_MODEL), ATTN_WIDTH ** -0.5),
        "w_out": n(ks[11], (DEPTH, D_MODEL, D_MODEL), D_MODEL ** -0.5),
        "norm_mlp": 1.0 + n(ks[12], (DEPTH, D_MODEL), 0.02),
        "w_up": n(ks[13], (DEPTH, D_MODEL, D_FF), D_MODEL ** -0.5),
        "w_down": n(ks[14], (DEPTH, D_FF, D_MODEL), D_FF ** -0.5),
        "norm_final": 1.0 + n(ks[15], (D_MODEL,), 0.02),
    }

def reference(x_prompt, x_sample, cache_k, cache_v, state_pool, norm_mix, w_in, sinks, w_pool, pool_scale,
              w_attn_up, w_out, norm_mlp, w_up, w_down, norm_final):
    hp = x_prompt
    hs = x_sample
    B, T = hp.shape[:2]
    Bd, Td = hs.shape[:2]
    pos_p = jnp.arange(T)
    pos_s = PAST_LEN + jnp.arange(Td)
    nk_p, nv_p, npool_p, nk_s, nv_s, npool_s = [], [], [], [], [], []
    for l in range(DEPTH):
        xp, q, k, v, gp, ga = _split_in(_rmsnorm(hp, norm_mix[l]) @ w_in[l])
        q = _rope(q.reshape(B, T, N_HEADS, HEAD_DIM), pos_p)
        k = _rope(k.reshape(B, T, N_KV_HEADS, HEAD_DIM), pos_p)
        v = v.reshape(B, T, N_KV_HEADS, HEAD_DIM)
        xx = jnp.concatenate([jnp.zeros((B, POOL_BUF, POOL_WIDTH), xp.dtype), xp], axis=1)
        pool_out = _pool_mix(xx, pos_p, w_pool[l], pool_scale[l])
        attn = _banded_attention(q, k, v, sinks[l])
        hp = hp + _merge(pool_out, attn, gp, ga, w_attn_up[l], w_out[l])
        hp = hp + _mlp(_rmsnorm(hp, norm_mlp[l]), w_up[l], w_down[l])
        keep = min(WINDOW, T)
        nk_p.append(k[:, T - keep:])
        nv_p.append(v[:, T - keep:])
        npool_p.append(xx[:, -POOL_BUF:])

        xps, qs, ks_, vs, gps, gas = _split_in(_rmsnorm(hs, norm_mix[l]) @ w_in[l])
        qs = _rope(qs.reshape(Bd, Td, N_HEADS, HEAD_DIM), pos_s)
        ks_ = _rope(ks_.reshape(Bd, Td, N_KV_HEADS, HEAD_DIM), pos_s)
        vs = vs.reshape(Bd, Td, N_KV_HEADS, HEAD_DIM)
        xxs = jnp.concatenate([state_pool[l], xps], axis=1)
        pool_s = _pool_mix(xxs, pos_s, w_pool[l], pool_scale[l])
        Lc = cache_k.shape[2]
        kall = jnp.concatenate([cache_k[l], ks_], axis=1)
        vall = jnp.concatenate([cache_v[l], vs], axis=1)
        kpos = PAST_LEN - Lc + jnp.arange(Lc + Td)
        mask = _win_mask(pos_s[:, None], kpos[None, :])[None]
        o = _sink_attention(qs.reshape(Bd, 1, Td, N_KV_HEADS, Q_GROUP, HEAD_DIM), kall[:, None], vall[:, None],
                            mask, sinks[l])
        attn_s = o.reshape(Bd, Td, ATTN_WIDTH)
        hs = hs + _merge(pool_s, attn_s, gps, gas, w_attn_up[l], w_out[l])
        hs = hs + _mlp(_rmsnorm(hs, norm_mlp[l]), w_up[l], w_down[l])
        nk_s.append(kall[:, -Lc:])
        nv_s.append(vall[:, -Lc:])
        npool_s.append(xxs[:, -POOL_BUF:])

    y_prompt = _rmsnorm(hp, norm_final)
    y_sample = _rmsnorm(hs, norm_final)
    return (y_prompt, y_sample, jnp.stack(nk_p), jnp.stack(nv_p), jnp.stack(npool_p),
            jnp.stack(nk_s), jnp.stack(nv_s), jnp.stack(npool_s))


_drawn_inputs = setup_inputs


def setup_inputs(seed=0):
    import zlib

    import numpy as np

    out = dict(_drawn_inputs(seed))
    spreads = {}
    factors = {'sinks': 8.0, 'pool_scale': 6.159, 'norm_mlp': 3.367, 'norm_final': 2.844}
    for name, (base, spread) in spreads.items():
        noise = np.random.default_rng([zlib.crc32(name.encode()), seed]).standard_normal(out[name].shape)
        drawn = base * np.exp(spread * noise) if base else spread * noise
        out[name] = __import__('jax').numpy.asarray(drawn.astype(out[name].dtype))
    for name, factor in factors.items():
        out[name] = (out[name] * factor).astype(out[name].dtype)
    return out
```

```python
from contextlib import ExitStack

import numpy as np
import concourse.bass as bass
from concourse import mybir

F32 = mybir.dt.float32
F32R = mybir.dt.float32r
ALU = mybir.AluOpType
ACT = mybir.ActivationFunctionType
AX = mybir.AxisListType.X

P = 128
D = 1024
KD = D // P
SEQ, DEC = 2048, 32
TB = 512
NB = SEQ // TB
CH = 64
NC = TB // CH
NT = TB // P
HD = 64
NJ = 4
KV = 2
G = 4
PBUF = 15
PAST = 2048
CACHE = 128
DFF = 4096
NQ = DFF // D
WIDTH = P * KD
CMAX = TB + DEC
XW = 16 + TB
XWMAX = XW + 16 + DEC
KEYS_S = DEC + CH
EPS = 1e-6
SCALE = HD ** -0.5
MASKED = -1e30

U_Q, U_XP, U_GP, U_POOL, U_AG, U_OUT, U_MLP = 0, 6, 10, 18, 20, 32, 40
UNITS = U_MLP + 2 * KD * NQ
M_Q, M_XP, M_GP, M_POOL, M_AG, M_OUT, M_MLP = 0, 6, 10, 18, 26, 42, 50
PRODS = M_MLP + 2 * KD * NQ
RAW, SPLIT = 4, 2
X_NORMS = ((), (), (0,), (1, 2), (3,), (4, 5), (6,), (7,))
ATT0 = 8
assert UNITS % RAW == 0 and PRODS % 2 == 0


def build(nc, x0, x123, weights, consts, vectors, tables, state_s, kcache_t, vcache, kold, vold,
          y0, y123, k_new, v_new, p_new, k_old_out, v_old_out, ks_new, vs_new, ps_new):
    with ExitStack() as ctx:
        def sb(name, shape, dt=F32):
            return ctx.enter_context(nc.sbuf_tensor(name, shape, dt))

        def sem(name):
            return ctx.enter_context(nc.semaphore(name))

        class Signal:

            def __init__(self, name, items):
                self.sem = sem(name)
                self.count = {item: n + 1 for n, item in enumerate(items)}

        def cols(b):
            return CMAX if b == 0 else TB

        def nchunks(b):
            return NC + 1 if b == 0 else NC

        xT = sb("xT", [P, KD, CMAX])
        hT = sb("hT", [P, KD, CMAX])
        nH, nL = sb("nH", [P, KD, CMAX], F32R), sb("nL", [P, KD, CMAX], F32R)
        midH, midL = sb("midH", [P, KD, CMAX], F32R), sb("midL", [P, KD, CMAX], F32R)
        attH, attL = sb("attH", [P, NJ, CMAX], F32R), sb("attL", [P, NJ, CMAX], F32R)
        qbuf = sb("qbuf", [P, NJ * CMAX])
        qC = qbuf[:, 0:NJ * TB].rearrange("p (c j n) -> p c j n", c=NC, j=NJ)
        qS = qbuf[:, NJ * TB:].rearrange("p (j n) -> p j n", j=NJ)
        upT = qbuf[:, :].rearrange("p (m n) -> p m n", m=NJ)
        kT = sb("kT", [P, CH + CMAX])
        vA = sb("vA", [P, NT, P])
        vB = sb("vB", [P, NT + 1, P])
        vS = sb("vS", [KEYS_S, P])
        kcT = sb("kcT", [P, CH])
        raw = sb("raw", [P, RAW, WIDTH])
        wH, wL = sb("wH", [P, SPLIT, WIDTH], F32R), sb("wL", [P, SPLIT, WIDTH], F32R)
        work = sb("work", [P, 4, CMAX])
        sq = sb("sq", [P, 2, XWMAX])
        acc = sb("acc", [P, CMAX])
        diag = sb("diag", [P, XWMAX])
        xb = sb("xb", [P, 3, XWMAX])
        carry = sb("carry", [P, G, 16])
        carry_s = sb("carry_s", [P, G, 16])
        state = sb("state", [P, G, 16])
        pr = sb("pr", [P, 2, 4 * P])
        prT = sb("prT", [P, 2, 4 * P])
        rope = sb("rope", [P, 2, CMAX])
        cst = sb("cst", [P, 2 * P + G * 16])
        ident, rot = cst[:, 0:P], cst[:, P:2 * P]
        head_scale = cst[:, 2 * P:].rearrange("p (g c) -> p g c", g=G)
        ones = sb("ones", [P, P])
        vec = sb("vec", [P, 4 * KD + 6])
        g_mix, p_scale, g_mlp, g_fin = (vec[:, i * KD:(i + 1) * KD] for i in range(4))
        half_scale = sb("half_scale", [P, KD])
        nsink = sb("nsink", [P, 6])
        small = sb("small", [P, 64])
        mask0, eps = small[:, 0:1], small[:, 1:2]
        std, rstd = small[:, 2:7], small[:, 7:12]
        smax, negm, sinkd, esink, rsum, den, rden = (small[:, 12 + 4 * i:16 + 4 * i] for i in range(7))

        prod = [ctx.enter_context(nc.psum_tensor(f"prod{i}", [P, 2, 512], F32)) for i in range(2)]
        auxA = ctx.enter_context(nc.psum_tensor("auxA", [P, 2, 512], F32))
        auxB = ctx.enter_context(nc.psum_tensor("auxB", [P, 2, 512], F32))

        def pview(t, b):
            return t[:, 0:2, 0:CMAX // 2] if b == 0 else t[:, 0:1, 0:TB]

        def sview(ap, b):
            return ap[:, 0:cols(b)].rearrange("p (s n) -> p s n", s=2 if b == 0 else 1)

        def f(ap):
            return ap.bitcast(F32)

        raw_in = [sem(f"raw_in{i}") for i in range(RAW)]
        const_in, x_in, rope_in = sem("const_in"), sem("x_in"), sem("rope_in")
        y_out = [sem("y_out0"), sem("y_out1")]
        kv_out, pool_out, copy_out = sem("kv_out"), sem("pool_out"), sem("copy_out")
        start = sem("start")
        w_high, w_low = sem("w_high"), sem("w_low")
        prod_done = sem("prod_done")
        relu_done, hid_sq = sem("relu_done"), sem("hid_sq")
        hid_high, hid_low = sem("hid_high"), sem("hid_low")
        down_added = sem("down_added")
        vec_chain, pool_chain = sem("vec_chain"), sem("pool_chain")

        norms = [("x", 0)]
        for b in range(NB):
            norms += [("h", b)] + ([("x", b + 1)] if b + 1 < NB else []) + [("f", b)]
        inner = [n for n in norms if n[0] != "f"]
        blocks = range(NB)
        s_sq = Signal("squared", [(*n, k) for n in norms for k in range(KD)])
        s_acc = Signal("squares_added", [(*n, k) for n in norms for k in range(1, KD)])
        s_stat = Signal("squares_summed", norms)
        s_std = Signal("root_taken", norms)
        s_rstd = Signal("root_inverted", norms)
        s_diag = Signal("rstd_on_diagonal", norms)
        s_bc = Signal("rstd_spread", norms)
        s_n = Signal("normed", [(*n, k) for n in inner for k in range(KD)])
        s_nH = Signal("normed_high", [(*n, k) for n in inner for k in range(KD)])
        s_nL = Signal("normed_low", [(*n, k) for n in inner for k in range(KD)])
        s_y = Signal("y_normed", [(b, k) for b in blocks for k in range(KD)])
        s_tmp = Signal("qkv_copied", [(b, i) for b in blocks for i in range(6)])
        s_rot = Signal("halves_swapped", [(b, i) for b in blocks for i in range(5)])
        s_q = Signal("rotated", [(b, i) for b in blocks for i in range(5)])
        s_vt = Signal("v_transposed", [(b,) for b in blocks])
        s_vA = Signal("vA_copied", [(b,) for b in blocks])
        s_vB = Signal("vB_copied", [(b,) for b in blocks])
        groups = [(b, g) for b in blocks for g in range(G)]
        s_xb = Signal("pool_in_copied", groups)
        s_carry = Signal("pool_carried", groups)
        s_p = Signal("pooled", groups)
        s_pH = Signal("pooled_high", groups)
        s_pL = Signal("pooled_low", groups)
        chunks = [(b, c) for b in blocks for c in range(nchunks(b))]
        s_sc = Signal("scores", chunks)
        s_negm = Signal("max_negated", chunks)
        s_exp = Signal("exps", chunks)
        s_prn = Signal("probs_normed", chunks)
        s_pt = Signal("probs_transposed", chunks)
        s_ptS = Signal("probs_copied", chunks)
        s_pv = Signal("values_mixed", chunks)
        s_aH = Signal("attn_high", chunks)
        s_aL = Signal("attn_low", chunks)
        tiles = [(b, m) for b in blocks for m in range(KD)]
        s_gp = Signal("pool_gate", tiles)
        s_pool = Signal("pool_gated", tiles)
        s_ao = Signal("attn_up", tiles)
        s_ga = Signal("attn_gate", tiles)
        s_gat = Signal("attn_gated", tiles)
        s_mrg = Signal("merged", tiles)
        s_mH = Signal("merged_high", tiles)
        s_mL = Signal("merged_low", tiles)
        s_h = Signal("h_added", tiles)

        def wait(eng, signal, *item):
            eng.wait_ge(signal.sem, signal.count[item])

        def product_of(i):
            if i < M_XP:
                return "qkv", i
            if i < M_GP:
                return "xp", i - M_XP
            if i < M_POOL:
                return "gp", i - M_GP
            if i < M_AG:
                return "pool", i - M_POOL
            if i < M_OUT:
                c, r = divmod(i - M_AG, 4)
                return ("ao" if r < 2 else "ga"), 2 * c + r % 2
            return "out", i - M_OUT

        def unit_of(i):
            kind, m = product_of(i)
            if kind == "pool":
                return U_POOL + m // 4, (m % 4) * P, m % 4 == 3
            if kind == "ao":
                return U_AG + 3 * (m // 2), (m % 2) * 4 * P, m % 2 == 1
            if kind == "ga":
                return U_AG + 3 * (m // 2) + 1 + m % 2, 0, True
            return (i if i < M_POOL else i - M_OUT + U_OUT), 0, True

        def wait_product(eng, b, i):
            eng.wait_ge(prod_done, b * PRODS + i + 1)

        def wait_mlp(eng, b, q, i):
            eng.wait_ge(prod_done, 16 * q + (b * PRODS + M_MLP + i + 1))

        def hid(b, q, m):
            return 8 * q + (b * KD * NQ + m + 1)

        def quarters(eng, b, up, down, last):
            up(b, 0)
            with eng.Fori(0, NQ - 1) as q:
                down(b, q)
                up(b, q + 1)
            last(b)

        block = ctx.enter_context(nc.Block())

        @block.sync
        def _(sp):
            def load_mixer_unit(b, u):
                n = b * UNITS + u
                if n >= RAW:
                    sp.wait_ge(w_low, n - RAW + 1)
                sp.dma_start(raw[:, n % RAW, :], weights[n % UNITS, :, :]).then_inc(raw_in[n % RAW], 16)

            def load_mlp_unit(b, q, i):
                sp.wait_ge(w_low, 16 * q + (b * UNITS + U_MLP + i - RAW + 1))
                sp.dma_start(raw[:, i % RAW, :], weights[16 * q + (U_MLP + i), :, :]).then_inc(raw_in[i % RAW], 16)

            def load_rope(b):
                if b > 0:
                    wait(sp, s_q, b - 1, 4)
                sp.dma_start(rope[:, :, 0:TB], tables[:, :, b * TB:(b + 1) * TB]).then_inc(rope_in, 16)
                if b == 0:
                    sp.dma_start(rope[:, :, TB:CMAX], tables[:, :, SEQ:SEQ + DEC]).then_inc(rope_in, 16)

            sp.dma_start(vec[:, :], vectors).then_inc(const_in, 16)
            sp.dma_start(cst[:, :], consts).then_inc(const_in, 16)
            for k in range(0, KD, 2):
                sp.dma_start(xT[:, k:k + 2, :], x0[:, k:k + 2, :]).then_inc(x_in, 16)
            for u in range(RAW):
                load_mixer_unit(0, u)
            load_rope(0)
            sp.dma_start(kcT[:, :], kcache_t).then_inc(const_in, 16)
            sp.dma_start(vS[DEC:KEYS_S, :], vcache).then_inc(const_in, 16)
            sp.dma_start(state[:, :, :], state_s).then_inc(const_in, 16)
            sp.dma_start(k_old_out, kold).then_inc(copy_out, 16)
            sp.dma_start(v_old_out, vold).then_inc(copy_out, 16)

            def up(b, q):
                for m in range(KD):
                    load_mlp_unit(b, q, m)
                    if isinstance(q, int) and m == 3 and b + 1 < NB:
                        wait(sp, s_h, b, KD - 1)
                        sp.dma_start(xT[:, :, 0:TB], x123[b, :, :, :]).then_inc(x_in, 16)
                        load_rope(b + 1)

            def down(b, q):
                for m in range(KD):
                    load_mlp_unit(b, q, KD + m)

            for b in blocks:
                for u in range(RAW if b == 0 else 0, U_MLP):
                    load_mixer_unit(b, u)
                quarters(sp, b, up, down, lambda b: down(b, NQ - 1))
            sp.wait_ge(copy_out, 32)

        @block.tensor
        def _(pe):
            def stream(out, b, lhs, rhs, first, last):
                for s, lo, hi in ((0, 0, 272), (1, 272, CMAX)) if b == 0 else ((0, 0, TB),):
                    ins = nc.tensor.matmul(out[:, s, 0:hi - lo], lhs, rhs[:, lo:hi], start=first, stop=last)
                return ins

            def product(b, slot, uslot, off, high, low, k0, nk, before_k=None):
                for i in range(nk):
                    if before_k:
                        before_k(k0 + i)
                    wh = wH[:, uslot, off + i * P:off + (i + 1) * P]
                    wl = wL[:, uslot, off + i * P:off + (i + 1) * P]
                    stream(prod[slot], b, wh, high[:, k0 + i, :], i == 0, False)
                    stream(prod[slot], b, wh, low[:, k0 + i, :], False, False)
                    ins = stream(prod[slot], b, wl, high[:, k0 + i, :], False, i == nk - 1)
                ins.then_inc(prod_done, 1)

            def wait_read(b, i):
                if i < 2:
                    if b > 0:
                        pe.wait_ge(down_added, hid(b - 1, NQ - 1, KD - 2 + i))
                    return
                kind, m = product_of(i - 2)
                signal = {"qkv": s_tmp, "xp": s_xb, "gp": s_gp, "pool": s_pool, "ao": s_ao, "ga": s_ga, "out": s_h}[kind]
                wait(pe, signal, b, m)

            def mixer_product(b, i):
                kind, m = product_of(i)
                u, off, _ = unit_of(i)
                wait_read(b, i)
                pe.wait_ge(w_low, b * UNITS + u + 1)
                before = None
                high, low, k0, nk = nH, nL, 0, KD
                if i == 0:
                    before = lambda k: wait(pe, s_nL, "x", b, k)
                if kind == "pool":
                    high, low, k0, nk = midH, midL, m // 2, 1
                    before = lambda g: wait(pe, s_pL, b, g)
                if kind == "ao":
                    high, low, nk = attH, attL, NJ
                    if m == 0:
                        wait(pe, s_aL, b, nchunks(b) - 1)
                if kind == "out":
                    high, low = midH, midL
                    if m == 0:
                        before = lambda k: wait(pe, s_mL, b, k)
                product(b, i % 2, (b * UNITS + u) % 2, off, high, low, k0, nk, before)

            def sum_squares(kind, b):
                wait(pe, s_acc, kind, b, KD - 1)
                for t in range(NT):
                    ins = nc.tensor.matmul(auxA[:, 1, t:t + 1], acc[:, t * P:(t + 1) * P], ones[:, 0:1],
                                           start=True, stop=True)
                if b == 0:
                    ins = nc.tensor.matmul(auxA[0:DEC, 1, NT:NT + 1], acc[:, TB:CMAX], ones[:, 0:1],
                                           start=True, stop=True)
                ins.then_inc(s_stat.sem, 1)

            def spread(kind, b):
                wait(pe, s_diag, kind, b)
                if b == 0:
                    nc.tensor.matmul(auxA[:, 0, 0:272], ones[:, :], diag[:, 0:272], start=True, stop=True)
                    nc.tensor.matmul(auxA[:, 1, 0:240], ones[:, :], diag[:, 272:TB], start=True, stop=True)
                    ins = nc.tensor.matmul(auxA[:, 1, 240:272], ones[0:DEC, :], diag[0:DEC, TB:CMAX],
                                           start=True, stop=True)
                else:
                    ins = nc.tensor.matmul(auxA[:, 0, :], ones[:, :], diag[:, 0:TB], start=True, stop=True)
                ins.then_inc(s_bc.sem, 1)

            def swap_halves(b, i):
                wait(pe, s_tmp, b, i)
                if i > 0:
                    wait(pe, s_q, b, i - 1)
                stream(auxB, b, rot, work[:, i % 2, :], True, True).then_inc(s_rot.sem, 1)

            def transpose_v(b):
                wait(pe, s_tmp, b, 5)
                if b > 0:
                    wait(pe, s_y, b - 1, KD - 1)
                for t in range(NT):
                    ins = nc.tensor.transpose(auxA[:, 1, t * P:(t + 1) * P], work[:, 1, t * P:(t + 1) * P], ident)
                if b == 0:
                    ins = nc.tensor.transpose(auxA[0:DEC, 0, 0:P], work[:, 1, TB:CMAX], ident)
                ins.then_inc(s_vt.sem, 1)

            def scores(b, c):
                if c >= 1:
                    wait(pe, s_exp, b, c - 1)
                else:
                    wait(pe, s_q, b, 4)
                    wait(pe, s_vA, b)
                for g in range(KV):
                    rows, bank = slice(g * HD, (g + 1) * HD), auxA[:, g, :]
                    if c == NC:
                        q = qbuf[rows, NJ * TB:]
                        nc.tensor.matmul(bank[:, 0:DEC], q, kT[rows, CH + TB:CH + CMAX],
                                         start=True, stop=True)
                        ins = nc.tensor.matmul(bank[:, DEC:KEYS_S], q, kcT[rows, :],
                                               start=True, stop=True)
                        continue
                    for pair in range(2):
                        at = pair * P
                        q = qbuf[rows, (4 * c + 2 * pair) * CH:(4 * c + 2 * pair + 2) * CH]
                        if c % 2:
                            ins = nc.tensor.matmul(bank[:, at:at + P], q, kT[rows, c * CH:(c + 2) * CH],
                                                   start=True, stop=True)
                        else:
                            nc.tensor.matmul(bank[:, at:at + CH], q, kT[rows, (c + 1) * CH:(c + 2) * CH],
                                             start=True, stop=True)
                            ins = nc.tensor.matmul(bank[:, at + CH:at + P], q, kT[rows, c * CH:(c + 1) * CH],
                                                   start=True, stop=True)
                ins.then_inc(s_sc.sem, 1)

            def transpose_probs(b, c):
                wait(pe, s_prn, b, c)
                if c >= 1:
                    wait(pe, s_ptS, b, c - 1)
                if c == NC:
                    for g in range(KV):
                        ins = nc.tensor.transpose(auxB[0:KEYS_S, 1, g * P:(g + 1) * P],
                                                  pr[:, 0, g * KEYS_S:(g + 1) * KEYS_S], ident)
                else:
                    for i in range(4):
                        ins = nc.tensor.transpose(auxB[:, 1, i * P:(i + 1) * P], pr[:, c % 2, i * P:(i + 1) * P], ident)
                ins.then_inc(s_pt.sem, 1)

            def mix_values(b, c):
                wait(pe, s_ptS, b, c)
                if c >= 1:
                    wait(pe, s_aL, b, c - 1)
                else:
                    wait(pe, s_vB, b)
                for g in range(KV):
                    feats = slice(g * HD, (g + 1) * HD)
                    if c == NC:
                        ins = nc.tensor.matmul(auxB[feats, 0, 0:P], vS[:, feats], prT[0:KEYS_S, 0, g * P:(g + 1) * P],
                                               start=True, stop=True)
                    else:
                        v = vA if c % 2 else vB
                        ins = nc.tensor.matmul(auxB[feats, 0, 0:2 * P], v[:, c // 2, feats],
                                               prT[:, c % 2, 2 * g * P:2 * (g + 1) * P], start=True, stop=True)
                ins.then_inc(s_pv.sem, 1)

            def between(b, i):
                if b > 0 and i == 0:
                    sum_squares("f", b - 1)
                if b > 0 and i == 1:
                    spread("f", b - 1)
                if 1 <= i <= 5:
                    swap_halves(b, i - 1)
                if i == 6:
                    transpose_v(b)
                if 0 <= i - ATT0 - 2 < nchunks(b):
                    mix_values(b, i - ATT0 - 2)
                if 0 <= i - ATT0 - 1 < nchunks(b):
                    transpose_probs(b, i - ATT0 - 1)
                if 0 <= i - ATT0 < nchunks(b):
                    scores(b, i - ATT0)

            def up(b, q):
                for m in range(KD):
                    first = isinstance(q, int) and q == 0
                    if m >= 2:
                        pe.wait_ge(relu_done, hid(b, q, m - 2))
                    elif first:
                        wait(pe, s_h, b, KD - 2 + m)
                    else:
                        pe.wait_ge(down_added, hid(b, q - 1, KD - 2 + m))
                    pe.wait_ge(w_low, 16 * q + (b * UNITS + U_MLP + m + 1))
                    before = (lambda k: wait(pe, s_nL, "h", b, k)) if first and m == 0 else None
                    product(b, m % 2, m % 2, 0, nH, nL, 0, KD, before)

            def down(b, q):
                for m in range(KD):
                    if m >= 2:
                        pe.wait_ge(down_added, hid(b, q, m - 2))
                    else:
                        pe.wait_ge(relu_done, hid(b, q, KD - 2 + m))
                    pe.wait_ge(w_low, 16 * q + (b * UNITS + U_MLP + KD + m + 1))
                    before = (lambda k: pe.wait_ge(hid_low, hid(b, q, k))) if m == 0 else None
                    product(b, m % 2, m % 2, 0, midH, midL, 0, KD, before)
                    if isinstance(q, int) and q == NQ - 1 and b + 1 < NB:
                        if m == 0:
                            sum_squares("x", b + 1)
                        if m == 1:
                            spread("x", b + 1)

            pe.wait_ge(const_in, 80)
            pe.wait_ge(start, 1)
            sum_squares("x", 0)
            spread("x", 0)
            for b in blocks:
                for i in range(M_MLP):
                    mixer_product(b, i)
                    between(b, i)
                sum_squares("h", b)
                spread("h", b)
                quarters(pe, b, up, down, lambda b: down(b, NQ - 1))
            sum_squares("f", NB - 1)
            spread("f", NB - 1)

        @block.scalar
        def _(act):
            def copy(out, in_, scale=1.0):
                return nc.scalar.activation(out, in_, ACT.Copy, scale=scale)

            def split_high(b, u):
                n = b * UNITS + u
                if n >= NB * UNITS:
                    return
                act.wait_ge(raw_in[n % RAW], 16 * (n // RAW + 1))
                copy(wH[:, n % 2, :], raw[:, n % RAW, :]).then_inc(w_high, 1)

            def split_high_mlp(b, q, i):
                n = b * UNITS + U_MLP + i
                act.wait_ge(raw_in[n % RAW], 64 * q + 16 * (n // RAW + 1))
                copy(wH[:, n % 2, :], raw[:, n % RAW, :]).then_inc(w_high, 1)

            def square(kind, b, k, src):
                at = norms.index((kind, b)) * (KD - 1)
                if k >= 2:
                    act.wait_ge(s_acc.sem, at + max(1, k - 2))
                elif at:
                    act.wait_ge(s_acc.sem, at)
                nc.scalar.activation(sview(sq[:, k % 2, :], b), sview(src[:, k, :], b), ACT.Square).then_inc(s_sq.sem, 1)

            def root(kind, b):
                wait(act, s_stat, kind, b)
                ins = nc.scalar.activation(std[:, 0:NT], auxA[:, 1, 0:NT], ACT.Sqrt, bias=eps, scale=1.0 / D)
                if b == 0:
                    ins = nc.scalar.activation(std[0:DEC, NT:NT + 1], auxA[0:DEC, 1, NT:NT + 1], ACT.Sqrt,
                                               bias=eps[0:DEC], scale=1.0 / D)
                ins.then_inc(s_std.sem, 1)

            def norm_high(kind, b, k):
                wait(act, s_n, kind, b, k)
                copy(nH[:, k, 0:cols(b)], work[:, k % 2, 0:cols(b)]).then_inc(s_nH.sem, 1)

            def exps(b, c):
                wait(act, s_negm, b, c)
                n, w = (KV, KEYS_S) if c == NC else (4, P)
                for i in range(n):
                    at = i % (n // KV) * w
                    nc.scalar.activation(pr[:, c % 2, i * w:(i + 1) * w], auxA[:, i * KV // n, at:at + w], ACT.Exp,
                                         bias=negm[:, i:i + 1], scale=SCALE, accum_out=rsum[:, i:i + 1])
                nc.scalar.activation(esink[:, 0:n], sinkd[:, 0:n], ACT.Exp).then_inc(s_exp.sem, 1)

            def copy_probs(b, c):
                wait(act, s_pt, b, c)
                if c == NC:
                    copy(prT[0:KEYS_S, 0, 0:2 * P], auxB[0:KEYS_S, 1, 0:2 * P]).then_inc(s_ptS.sem, 1)
                else:
                    copy(prT[:, c % 2, :], auxB[:, 1, :]).then_inc(s_ptS.sem, 1)

            def attn_high(b, c):
                wait(act, s_pv, b, c)
                w = DEC if c == NC else CH
                copy(attH[:, :, c * CH:c * CH + w],
                     auxB[:, 0, 0:NJ * w].rearrange("p (j n) -> p j n", j=NJ)).then_inc(s_aH.sem, 1)

            def read_out(b, i):
                kind, m = product_of(i)
                wait_product(act, b, i) if kind not in ("pool", "out") else None
                src = pview(prod[i % 2], b)
                if kind == "qkv":
                    if m >= 2:
                        wait(act, s_q, b, m - 2)
                    copy(sview(work[:, m % 2, :], b), src).then_inc(s_tmp.sem, 1)
                if kind == "xp":
                    if m == 3:
                        wait(act, s_p, b, 0)
                    elif b > 0:
                        wait(act, s_p, b - 1, 3 if m == 0 else m)
                    to = xb[:, m % 3, :]
                    if b == 0:
                        copy(to[:, 16:16 + 272], src[:, 0, :])
                        copy(to[:, 16 + 272:XW], src[:, 1, 0:240])
                        copy(to[:, XWMAX - DEC:XWMAX], src[:, 1, 240:272]).then_inc(s_xb.sem, 1)
                    else:
                        copy(to[:, 16:XW], src[:, 0, :]).then_inc(s_xb.sem, 1)
                if kind == "gp":
                    if b > 0:
                        act.wait_ge(y_out[m // 4], 16 * b)
                    nc.scalar.activation(sview(hT[:, m, :], b), src, ACT.Tanh, scale=0.5).then_inc(s_gp.sem, 1)
                if kind == "ao":
                    if m >= 4:
                        wait(act, s_gat, b, m - 4)
                    copy(sview(upT[:, m % 4, :], b), src, 0.5).then_inc(s_ao.sem, 1)
                if kind == "ga":
                    if m >= 2:
                        wait(act, s_gat, b, m - 2)
                    elif m == 1 and b in (0, NB - 1):
                        act.wait_ge(kv_out, 32 if b == 0 else 64)
                    nc.scalar.activation(sview(work[:, m % 2, :], b), src, ACT.Tanh, scale=0.5).then_inc(s_ga.sem, 1)

            def merged_high(b, m):
                wait(act, s_mrg, b, m)
                copy(midH[:, m, 0:cols(b)], hT[:, m, 0:cols(b)]).then_inc(s_mH.sem, 1)

            def pooled_high(b, g):
                wait(act, s_p, b, g)
                ins = copy(midH[:, g, 0:TB], diag[:, 16:XW])
                if b == 0:
                    ins = copy(midH[:, g, TB:CMAX], diag[:, XWMAX - DEC:XWMAX])
                ins.then_inc(s_pH.sem, 1)

            def store_y(b, half):
                wait(act, s_y, b, 4 * half + 3)
                ks = slice(4 * half, 4 * half + 4)
                dst = y0[:, ks, :] if b == 0 else y123[b - 1, :, ks, :]
                act.dma_start(dst, hT[:, ks, 0:cols(b)]).then_inc(y_out[half], 16)

            def step(b, i):
                kind, m = product_of(i)
                read_out(b, i)
                u, _, last_of_unit = unit_of(i)
                if b > 0 and i == 0:
                    root("f", b - 1)
                if b > 0 and i in (3, 5):
                    store_y(b - 1, (i - 3) // 2)
                if i == 6:
                    wait(act, s_vt, b)
                    if b == 0:
                        copy(vS[0:DEC, :], auxA[0:DEC, 0, 0:P])
                    copy(vA[:, :, :], auxA[:, 1, :].rearrange("p (t f) -> p t f", t=NT)).then_inc(s_vA.sem, 1)
                    if b == 0:
                        wait(act, s_q, b, 4)
                        act.dma_start(ks_new, kT[:, CH + TB:CH + CMAX]).then_inc(kv_out, 16)
                        wait(act, s_tmp, b, 5)
                        act.dma_start(vs_new, work[:, 1, TB:CMAX]).then_inc(kv_out, 16)
                    if b == NB - 1:
                        wait(act, s_q, b, 4)
                        act.dma_start(k_new, kT[:, CH + TB - P:CH + TB]).then_inc(kv_out, 16)
                        wait(act, s_tmp, b, 5)
                        act.dma_start(v_new, work[:, 1, TB - P:TB]).then_inc(kv_out, 16)
                if 0 <= i - ATT0 - 2 < nchunks(b):
                    attn_high(b, i - ATT0 - 2)
                if 0 <= i - ATT0 - 1 < nchunks(b):
                    copy_probs(b, i - ATT0 - 1)
                if kind == "out" and m >= 1:
                    wait(act, s_h, b, m - 1)
                    square("h", b, m - 1, hT)
                if last_of_unit:
                    wait_product(act, b, i)
                    split_high(b, u + 2)
                if kind == "ga":
                    merged_high(b, m)
                if 0 <= i - ATT0 < nchunks(b):
                    exps(b, i - ATT0)
                if i in (8, 10, 12, 15):
                    pooled_high(b, (8, 10, 12, 15).index(i))
                if i == 20 and b in (0, NB - 1):
                    wait(act, s_carry, b, G - 1)
                    if b == 0:
                        act.dma_start(ps_new, carry_s[:, :, :]).then_inc(pool_out, 16)
                    else:
                        act.dma_start(p_new, carry[:, :, :]).then_inc(pool_out, 16)

            def up(b, q):
                first = isinstance(q, int) and q == 0
                for m in range(KD):
                    wait_mlp(act, b, q, m)
                    if not (b == 0 and first and m < 2):
                        act.wait_ge(hid_sq, hid(b, q, m - 2))
                    nc.scalar.activation(sview(work[:, m % 2, :], b), pview(prod[m % 2], b), ACT.Relu).then_inc(relu_done, 1)
                    split_high_mlp(b, q, m + 2)
                    act.wait_ge(relu_done, hid(b, q, m))
                    nc.scalar.activation(midH[:, m, 0:cols(b)], work[:, m % 2, 0:cols(b)], ACT.Square).then_inc(hid_high, 1)
                    if first and b + 1 < NB and m >= 4:
                        if m == 4:
                            act.wait_ge(x_in, 64 + 16 * (b + 1))
                        square("x", b + 1, 2 * m - 8, xT)
                        square("x", b + 1, 2 * m - 7, xT)

            def down(b, q):
                for m in range(KD):
                    wait_mlp(act, b, q, KD + m)
                    split_high_mlp(b, q, KD + m + 2)

            def last_down(b):
                for m in range(KD):
                    wait_mlp(act, b, NQ - 1, KD + m)
                    split_high(b, UNITS - KD + m + 2)
                    act.wait_ge(down_added, hid(b, NQ - 1, m))
                    square("f", b, m, hT)
                    if b + 1 < NB and m == 0:
                        root("x", b + 1)
                    for k in X_NORMS[m] if b + 1 < NB else ():
                        norm_high("x", b + 1, k)

            act.wait_ge(start, 1)
            act.wait_ge(x_in, 64)
            for k in range(KD):
                square("x", 0, k, xT)
            root("x", 0)
            split_high(0, 0)
            split_high(0, 1)
            for k in range(KD):
                norm_high("x", 0, k)
            for b in blocks:
                for i in range(M_MLP):
                    step(b, i)
                wait(act, s_h, b, KD - 1)
                square("h", b, KD - 1, hT)
                root("h", b)
                for k in range(KD):
                    norm_high("h", b, k)
                quarters(act, b, up, down, last_down)
            root("f", NB - 1)
            store_y(NB - 1, 0)
            store_y(NB - 1, 1)
            for half in range(2):
                act.wait_ge(y_out[half], 16 * NB)
            act.wait_ge(kv_out, 64)
            act.wait_ge(pool_out, 32)

        @block.vector
        def _(dve):
            tt, stt = nc.vector.tensor_tensor, nc.vector.scalar_tensor_tensor
            chain = [0]

            def link(ins):
                chain[0] += 1
                ins.then_inc(vec_chain, 1)
                dve.wait_ge(vec_chain, chain[0])

            def low(out, x, high):
                return tt(out, x, f(high), ALU.subtract)

            def split_low(b, u):
                n = b * UNITS + u
                if n >= NB * UNITS:
                    return
                dve.wait_ge(w_high, n + 1)
                low(wL[:, n % 2, :], raw[:, n % RAW, :], wH[:, n % 2, :]).then_inc(w_low, 1)

            def split_low_mlp(b, q, i):
                n = b * UNITS + U_MLP + i
                dve.wait_ge(w_high, 16 * q + (n + 1))
                low(wL[:, n % 2, :], raw[:, n % RAW, :], wH[:, n % 2, :]).then_inc(w_low, 1)

            def add_square(kind, b, k):
                wait(dve, s_sq, kind, b, k)
                n = cols(b)
                if k == 1:
                    tt(acc[:, 0:n], sq[:, 0, 0:n], sq[:, 1, 0:n], ALU.add).then_inc(s_acc.sem, 1)
                elif k > 1:
                    wait(dve, s_acc, kind, b, k - 1)
                    tt(acc[:, 0:n], acc[:, 0:n], sq[:, k % 2, 0:n], ALU.add).then_inc(s_acc.sem, 1)

            def invert(kind, b):
                wait(dve, s_std, kind, b)
                ins = nc.vector.reciprocal(rstd[:, 0:NT], std[:, 0:NT])
                if b == 0:
                    ins = nc.vector.reciprocal(rstd[0:DEC, NT:NT + 1], std[0:DEC, NT:NT + 1])
                ins.then_inc(s_rstd.sem, 1)
                wait(dve, s_rstd, kind, b)
                ins = tt(diag[:, 0:TB].rearrange("p (t n) -> p t n", t=NT),
                         ident.unsqueeze(1).to_broadcast([P, NT, P]),
                         rstd[:, 0:NT].unsqueeze(2).to_broadcast([P, NT, P]), ALU.mult)
                if b == 0:
                    ins = tt(diag[0:DEC, TB:CMAX], ident[0:DEC, 0:DEC],
                             rstd[0:DEC, NT:NT + 1].to_broadcast([DEC, DEC]), ALU.mult)
                ins.then_inc(s_diag.sem, 1)

            def norm(kind, b, k, src, gain):
                if k == 0:
                    wait(dve, s_bc, kind, b)
                if k >= 2:
                    wait(dve, s_nL, kind, b, k - 2)
                stt(out=sview(work[:, k % 2, :], b), in0=sview(src[:, k, :], b), scalar=gain[:, k:k + 1],
                    in1=pview(auxA, b), op0=ALU.mult, op1=ALU.mult).then_inc(s_n.sem, 1)

            def norm_low(kind, b, k):
                wait(dve, s_nH, kind, b, k)
                n = cols(b)
                low(nL[:, k, 0:n], work[:, k % 2, 0:n], nH[:, k, 0:n]).then_inc(s_nL.sem, 1)

            def final(b, k):
                if k == 0:
                    wait(dve, s_bc, "f", b)
                stt(out=sview(hT[:, k, :], b), in0=sview(hT[:, k, :], b), scalar=g_fin[:, k:k + 1],
                    in1=pview(auxA, b), op0=ALU.mult, op1=ALU.mult).then_inc(s_y.sem, 1)

            def rotate(b, i):
                n = cols(b)
                if i == 0:
                    dve.wait_ge(rope_in, 16 * (b + 2))
                wait(dve, s_tmp, b, i)
                tt(work[:, 2, 0:n], work[:, i % 2, 0:n], rope[:, 0, 0:n], ALU.mult)
                wait(dve, s_rot, b, i)
                link(tt(sview(work[:, 3, :], b), pview(auxB, b), sview(rope[:, 1, :], b), ALU.mult))
                if i == NJ:
                    ins = tt(kT[:, CH:CH + n], work[:, 2, 0:n], work[:, 3, 0:n], ALU.add)
                else:
                    by_chunk = lambda j: work[:, j, 0:TB].rearrange("p (c n) -> p c n", c=NC)
                    ins = tt(qC[:, :, i, :], by_chunk(2), by_chunk(3), ALU.add)
                    if b == 0:
                        ins = tt(qS[:, i, :], work[:, 2, TB:CMAX], work[:, 3, TB:CMAX], ALU.add)
                ins.then_inc(s_q.sem, 1)
                wait(dve, s_q, b, i)

            def row_max(b, c):
                wait(dve, s_sc, b, c)
                n, w = (KV, KEYS_S) if c == NC else (4, P)
                sc = auxA[:, :, 0:n // KV * w].rearrange("p g (i k) -> p g i k", k=w)
                sink = nsink[:, 4:6] if c == NC else nsink[:, 0:4]
                if b == 0 and c == 0:
                    link(nc.vector.tensor_scalar(sc[:, :, :, CH:P], sc[:, :, :, CH:P], MASKED, None, ALU.add))
                link(nc.vector.tensor_reduce(smax[:, 0:n].rearrange("p (g i) -> p g i", g=KV), sc, AX, ALU.max))
                link(stt(out=negm[:, 0:n], in0=smax[:, 0:n], scalar=-SCALE, in1=sink, op0=ALU.mult, op1=ALU.min))
                tt(sinkd[:, 0:n], negm[:, 0:n], sink, ALU.subtract).then_inc(s_negm.sem, 1)

            def norm_probs(b, c):
                wait(dve, s_exp, b, c)
                n, w = (KV, KEYS_S) if c == NC else (4, P)
                link(tt(den[:, 0:n], rsum[:, 0:n], esink[:, 0:n], ALU.add))
                link(nc.vector.reciprocal(rden[:, 0:n], den[:, 0:n]))
                p = pr[:, c % 2, 0:n * w].rearrange("p (i k) -> p i k", i=n)
                tt(p, p, rden[:, 0:n].unsqueeze(2).to_broadcast([P, n, w]), ALU.mult).then_inc(s_prn.sem, 1)

            def attn_low(b, c):
                wait(dve, s_aH, b, c)
                w = DEC if c == NC else CH
                at = slice(c * CH, c * CH + w)
                low(attL[:, :, at], auxB[:, 0, 0:NJ * w].rearrange("p (j n) -> p j n", j=NJ),
                    attH[:, :, at]).then_inc(s_aL.sem, 1)

            def step(b, i):
                kind, m = product_of(i)
                n = cols(b)
                src = pview(prod[i % 2], b)
                if kind == "pool":
                    wait_product(dve, b, i)
                    wait(dve, s_gp, b, m)
                    stt(out=sview(hT[:, m, :], b), in0=sview(hT[:, m, :], b), scalar=1.0, in1=src,
                        op0=ALU.add, op1=ALU.mult).then_inc(s_pool.sem, 1)
                if kind == "out":
                    wait_product(dve, b, i)
                    tt(sview(hT[:, m, :], b), sview(xT[:, m, :], b), src, ALU.add).then_inc(s_h.sem, 1)
                if kind == "ga":
                    wait(dve, s_ga, b, m)
                    stt(out=work[:, 2 + m % 2, 0:n], in0=work[:, m % 2, 0:n], scalar=1.0, in1=upT[:, m % 4, 0:n],
                        op0=ALU.add, op1=ALU.mult).then_inc(s_gat.sem, 1)
                    wait(dve, s_gat, b, m)
                    stt(out=hT[:, m, 0:n], in0=hT[:, m, 0:n], scalar=half_scale[:, m:m + 1],
                        in1=work[:, 2 + m % 2, 0:n], op0=ALU.mult, op1=ALU.add).then_inc(s_mrg.sem, 1)
                if b > 0 and i == 0:
                    link(nc.vector.tensor_copy(kT[:, 0:CH], kT[:, TB:TB + CH]))
                    add_square("f", b - 1, KD - 1)
                    invert("f", b - 1)
                if i == 6:
                    wait(dve, s_vA, b)
                    if b > 0:
                        link(nc.vector.tensor_copy(vB[CH:P, 0, :], vB[CH:P, NT, :]))
                    nc.vector.tensor_copy(vB[0:CH, 0:NT, :], vA[0:CH, :, :])
                    nc.vector.tensor_copy(vB[CH:P, 1:NT + 1, :], vA[CH:P, :, :]).then_inc(s_vB.sem, 1)
                if 0 <= i - ATT0 - 2 < nchunks(b):
                    attn_low(b, i - ATT0 - 2)
                if 0 <= i - ATT0 < nchunks(b):
                    row_max(b, i - ATT0)
                u, _, last_of_unit = unit_of(i)
                if last_of_unit:
                    split_low(b, u + 2)
                if kind == "out" and m >= 2:
                    add_square("h", b, m - 1)
                if kind == "ga":
                    wait(dve, s_mH, b, m)
                    low(midL[:, m, 0:n], hT[:, m, 0:n], midH[:, m, 0:n]).then_inc(s_mL.sem, 1)
                if 1 <= i <= 5:
                    rotate(b, i - 1)
                if b > 0 and 1 <= i <= 4:
                    final(b - 1, 2 * i - 2)
                    final(b - 1, 2 * i - 1)
                if 0 <= i - ATT0 < nchunks(b):
                    norm_probs(b, i - ATT0)

            def up(b, q):
                first = isinstance(q, int) and q == 0
                n = cols(b)
                for m in range(KD):
                    dve.wait_ge(relu_done, hid(b, q, m))
                    tt(work[:, 2 + m % 2, 0:n], work[:, m % 2, 0:n], work[:, m % 2, 0:n], ALU.mult).then_inc(hid_sq, 1)
                    split_low_mlp(b, q, m + 2)
                    dve.wait_ge(hid_high, hid(b, q, m))
                    dve.wait_ge(hid_sq, hid(b, q, m))
                    low(midL[:, m, 0:n], work[:, 2 + m % 2, 0:n], midH[:, m, 0:n]).then_inc(hid_low, 1)
                    if first and b + 1 < NB and m >= 4:
                        add_square("x", b + 1, 2 * m - 8)
                        add_square("x", b + 1, 2 * m - 7)

            def add_down(b, q, m):
                wait_mlp(dve, b, q, KD + m)
                tt(sview(hT[:, m, :], b), sview(hT[:, m, :], b), pview(prod[m % 2], b), ALU.add).then_inc(down_added, 1)

            def down(b, q):
                for m in range(KD):
                    add_down(b, q, m)
                    split_low_mlp(b, q, KD + m + 2)

            def last_down(b):
                for m in range(KD):
                    add_down(b, NQ - 1, m)
                    split_low(b, UNITS - KD + m + 2)
                    if m >= 2:
                        add_square("f", b, m - 1)
                    if b + 1 < NB and m == 0:
                        invert("x", b + 1)
                    for k in X_NORMS[m] if b + 1 < NB else ():
                        norm("x", b + 1, k, xT, g_mix)
                        norm_low("x", b + 1, k)

            def norm_all(kind, b, src, gain):
                for k in range(KD + 1):
                    if k < KD:
                        norm(kind, b, k, src, gain)
                    if k >= 1:
                        norm_low(kind, b, k - 1)

            dve.wait_ge(const_in, 80)
            dve.wait_ge(start, 1)
            nc.vector.tensor_scalar(half_scale[:, :], p_scale, 0.5, None, ALU.mult)
            link(nc.vector.tensor_scalar(nsink[:, :], vec[:, 4 * KD:4 * KD + 6], -1.0, None, ALU.mult))
            for k in range(KD):
                add_square("x", 0, k)
            invert("x", 0)
            split_low(0, 0)
            norm_all("x", 0, xT, g_mix)
            split_low(0, 1)
            for b in blocks:
                for i in range(M_MLP):
                    step(b, i)
                add_square("h", b, KD - 1)
                invert("h", b)
                norm_all("h", b, hT, g_mlp)
                quarters(dve, b, up, down, last_down)
            add_square("f", NB - 1, KD - 1)
            invert("f", NB - 1)
            for k in range(KD):
                final(NB - 1, k)

        @block.gpsimd
        def _(pool):
            tt = nc.gpsimd.tensor_tensor

            def link(ins):
                chain[0] += 1
                ins.then_inc(pool_chain, 1)
                pool.wait_ge(pool_chain, chain[0])

            chain = [0]
            link(nc.gpsimd.memset(ones[:, :], 1.0))
            link(nc.gpsimd.memset(eps, EPS))
            link(nc.gpsimd.memset(kT[:, 0:CH], 0.0))
            nc.gpsimd.memset(vB[CH:P, 0, :], 0.0).then_inc(start, 1)
            pool.wait_ge(start, 1)
            pool.wait_ge(const_in, 80)
            for b in blocks:
                w = XWMAX if b == 0 else XW
                if b > 0:
                    wait(pool, s_acc, "f", b - 1, KD - 1)
                    wait(pool, s_bc, "f", b - 1)
                for g in range(G):
                    x = xb[:, g % 3, :]
                    wait(pool, s_xb, b, g)
                    if b > 0:
                        wait(pool, s_carry, b - 1, g)
                    link(nc.gpsimd.tensor_copy(x[:, 0:16], carry[:, g, :]) if b > 0 else nc.gpsimd.memset(x[:, 0:16], 0.0))
                    if b == 0:
                        link(nc.gpsimd.tensor_copy(x[:, XW:XW + 16], state[:, g, :]))
                        link(nc.gpsimd.tensor_copy(carry_s[:, g, :], x[:, XWMAX - 16:XWMAX]))
                    nc.gpsimd.tensor_copy(carry[:, g, :], x[:, XW - 16:XW]).then_inc(s_carry.sem, 1)
                    src = x
                    for s in range(g + 1):
                        lo, dst = 2 ** (s + 1) - 1, sq[:, s % 2, :]
                        link(tt(dst[:, lo:w], src[:, lo:w], src[:, lo - 2 ** s:w - 2 ** s], ALU.add))
                        src = dst
                    link(nc.gpsimd.tensor_scalar(diag[:, 16:w], src[:, 16:w], 1.0 / 2 ** (g + 1), None, ALU.mult))
                    if b == 0:
                        link(tt(diag[:, 16:32], src[:, 16:32], head_scale[:, g, :], ALU.mult))
                    tt(diag[:, 16:w], diag[:, 16:w], x[:, 16:w], ALU.subtract).then_inc(s_p.sem, 1)
                    wait(pool, s_pH, b, g)
                    ins = tt(midL[:, g, 0:TB], diag[:, 16:XW], f(midH[:, g, 0:TB]), ALU.subtract)
                    if b == 0:
                        ins = tt(midL[:, g, TB:CMAX], diag[:, XWMAX - DEC:XWMAX], f(midH[:, g, TB:CMAX]), ALU.subtract)
                    ins.then_inc(s_pL.sem, 1)


def constants():
    eye = np.eye(P, dtype=np.float32)
    rot = np.zeros((P, P), np.float32)
    half = HD // 8
    for head in range(0, P, HD):
        for i in range(half):
            rot[head + half + i, head + i] = -1.0
            rot[head + i, head + half + i] = 1.0
    head = np.stack([1.0 / np.minimum(np.arange(16) + 1, 2 ** (g + 1)) for g in range(G)]).astype(np.float32)
    consts = np.concatenate([eye, rot, np.tile(head.reshape(1, -1), (P, 1))], axis=1)
    inv = (np.float32(500000.0) ** (-np.arange(0, 2 * half, 2, dtype=np.float32) / np.float32(2 * half))).astype(np.float32)
    pos = np.concatenate([np.arange(SEQ), PAST + np.arange(DEC)]).astype(np.float32)
    angle = (pos[None, :] * inv[:, None]).astype(np.float32).astype(np.float64)
    tables = np.zeros((P, 2, SEQ + DEC), np.float32)
    tables[:, 0, :] = 1.0
    for at in range(0, P, half):
        if at % HD < 2 * half:
            tables[at:at + half, 0, :] = np.cos(angle)
            tables[at:at + half, 1, :] = np.sin(angle)
    return consts, tables


def unit_layout(w_in, w_pool, w_attn_up, w_out, w_up, w_down):
    def tile(w, cols):
        rows = w.shape[0] // P
        return w[:, cols].reshape(rows, P, P).transpose(1, 0, 2).reshape(P, rows * P)

    def cols(at):
        return np.arange(at, at + P)

    q0, k0 = G * P, G * P + NJ * KV * HD
    gp0 = k0 + 2 * P
    ga0 = gp0 + D
    units = []
    for j in range(NJ):
        units.append(tile(w_in, np.concatenate([np.arange(q0 + (g * NJ + j) * HD, q0 + (g * NJ + j + 1) * HD)
                                                for g in range(KV)])))
    units += [tile(w_in, cols(k0)), tile(w_in, cols(k0 + P))]
    units += [tile(w_in, cols(g * P)) for g in range(G)]
    units += [tile(w_in, cols(gp0 + m * P)) for m in range(KD)]
    pooled = w_pool.transpose(1, 0, 2).reshape(P, 2 * G * P)
    for half in range(2):
        units.append(np.concatenate([pooled[:, half * 512:(half + 1) * 512], np.zeros((P, 512), np.float32)], axis=1))
    up_rows = w_attn_up.reshape(KV, NJ, HD, D).transpose(1, 0, 2, 3).reshape(NJ * P, D)
    for c in range(KD // 2):
        units.append(np.concatenate([tile(up_rows, cols((2 * c + r) * P)) for r in range(2)], axis=1))
        units += [tile(w_in, cols(ga0 + (2 * c + r) * P)) for r in range(2)]
    units += [tile(w_out, cols(m * P)) for m in range(KD)]
    for q in range(NQ):
        units += [tile(w_up, cols(q * D + m * P)) for m in range(KD)]
        units += [tile(w_down[q * D:(q + 1) * D], cols(m * P)) for m in range(KD)]
    return np.ascontiguousarray(np.stack(units))


def feature_major(x):
    return np.ascontiguousarray(x.T.reshape(KD, P, -1).transpose(1, 0, 2))


def token_major(y):
    return y.transpose(1, 0, 2).reshape(D, -1).T


def kernel(x_prompt, x_sample, cache_k, cache_v, state_pool, norm_mix, w_in, sinks, w_pool, pool_scale,
           w_attn_up, w_out, norm_mlp, w_up, w_down, norm_final):
    import concourse.bacc as bacc
    from concourse.bass_utils import run_bass_kernel_spmd

    f32 = lambda a: np.asarray(a)
    xp, xs = f32(x_prompt)[0], f32(x_sample)[0]
    consts, tables = constants()
    by_tile = lambda v: f32(v).reshape(KD, P).T
    s = f32(sinks)[0].reshape(KV, NJ)
    rows = np.arange(P)
    sink_cols = [s[g, 2 * pair + rows // CH] for g in range(KV) for pair in range(2)]
    sink_cols += [s[g, rows // DEC] for g in range(KV)]
    vectors = np.concatenate([by_tile(norm_mix[0]), by_tile(pool_scale[0]), by_tile(norm_mlp[0]), by_tile(norm_final),
                              np.stack(sink_cols, axis=1)], axis=1)
    ck, cv = (f32(c)[0, 0].reshape(CACHE, P) for c in (cache_k, cache_v))
    hist = f32(state_pool)[0, 0].T.reshape(G, P, PBUF).transpose(1, 0, 2)
    arrays = {
        "x0": feature_major(np.concatenate([xp[:TB], xs])),
        "x123": np.stack([feature_major(xp[b * TB:(b + 1) * TB]) for b in range(1, NB)]),
        "weights": unit_layout(*(f32(w)[0] for w in (w_in, w_pool, w_attn_up, w_out, w_up, w_down))),
        "consts": consts, "vectors": vectors, "tables": tables,
        "state_s": np.concatenate([np.zeros((P, G, 1), np.float32), hist], axis=2),
        "kcache_t": ck[CACHE - CH:].T, "vcache": cv[CACHE - CH:],
        "kold": ck[DEC:], "vold": cv[DEC:],
    }
    arrays = {n: np.ascontiguousarray(a) for n, a in arrays.items()}
    outs = {"y0": (P, KD, CMAX), "y123": (NB - 1, P, KD, TB), "k_new": (P, P), "v_new": (P, P), "p_new": (P, G, 16),
            "k_old_out": (CACHE - DEC, P), "v_old_out": (CACHE - DEC, P), "ks_new": (P, DEC), "vs_new": (P, DEC),
            "ps_new": (P, G, 16)}
    nc = bacc.Bacc("TRN2", target_bir_lowering=False, num_devices=1)
    args = [nc.dram_tensor(n, a.shape, F32, kind="ExternalInput").ap() for n, a in arrays.items()]
    args += [nc.dram_tensor(n, shape, F32, kind="ExternalOutput").ap() for n, shape in outs.items()]
    build(nc, *args)
    got = run_bass_kernel_spmd(nc, [arrays], core_ids=[0]).results[0]

    first = token_major(got["y0"])
    rest = [token_major(got["y123"][b]) for b in range(NB - 1)]
    heads = lambda a: np.ascontiguousarray(a).reshape(1, 1, CACHE, KV, HD)
    tail = lambda a: np.ascontiguousarray(a[:, :, 1:].transpose(2, 1, 0)).reshape(1, 1, PBUF, G * P)
    return (np.concatenate([first[:TB], *rest])[None], first[TB:][None],
            heads(got["k_new"].T), heads(got["v_new"].T), tail(got["p_new"]),
            heads(np.concatenate([got["k_old_out"], got["ks_new"].T])),
            heads(np.concatenate([got["v_old_out"], got["vs_new"].T])),
            tail(got["ps_new"]))
```

```python
from contextlib import ExitStack

import numpy as np
import concourse.bass as bass
from concourse import mybir

F32 = mybir.dt.float32
F32R = mybir.dt.float32r
ALU = mybir.AluOpType
ACT = mybir.ActivationFunctionType
AX = mybir.AxisListType.X

P = 128
D = 1024
KD = D // P
SEQ, DEC = 2048, 32
TB = 512
NB = SEQ // TB
CH = 64
NC = TB // CH
NT = TB // P
HD = 64
NJ = 4
KV = 2
G = 4
PBUF = 15
PAST = 2048
CACHE = 128
DFF = 4096
NQ = DFF // D
WIDTH = P * KD
CMAX = TB + DEC
XW = 16 + TB
XWMAX = XW + 16 + DEC
KEYS_S = DEC + CH
EPS = 1e-6
SCALE = HD ** -0.5
MASKED = -1e30



def mixer_plan():
    plan = [("qkv", m) for m in range(6)] + [("xp", m) for m in range(G)] + [("gp", m) for m in range(KD)]
    for m in range(KD):
        plan += [("ga", m), ("ao", m)]
    return plan + [("out", m) for m in range(KD)]


MIXER = mixer_plan()
M_MLP = len(MIXER)
UNITS = M_MLP + 2 * KD * NQ
AO_WIDTH = (NJ + 1) * P
RAW, SPLIT = 4, 2
assert UNITS % 2 == 0 and M_MLP % 2 == 0 and 2 * KD % RAW == 0
ROPE_LOAD = 16
POOLED = KD - G
ATT0 = 7


def build(nc, x0, x123, weights, consts, vectors, tables, state_s, kcache_t, vcache, kold, vold,
          y0, y123, k_new, v_new, p_new, k_old_out, v_old_out, ks_new, vs_new, ps_new):
    with ExitStack() as ctx:
        def sb(name, shape, dt=F32):
            return ctx.enter_context(nc.sbuf_tensor(name, shape, dt))

        def sem(name):
            return ctx.enter_context(nc.semaphore(name))

        class Signal:

            def __init__(self, name, items):
                self.sem = sem(name)
                self.count = {item: n + 1 for n, item in enumerate(items)}

        def cols(b):
            return CMAX if b == 0 else TB

        def nchunks(b):
            return NC + 1 if b == 0 else NC

        xT = sb("xT", [P, KD, CMAX])
        hT = sb("hT", [P, KD, CMAX])
        nH, nL = sb("nH", [P, KD, CMAX], F32R), sb("nL", [P, KD, CMAX], F32R)
        midH, midL = sb("midH", [P, KD, CMAX], F32R), sb("midL", [P, KD, CMAX], F32R)
        attH, attL = sb("attH", [P, NJ, CMAX], F32R), sb("attL", [P, NJ, CMAX], F32R)
        qbuf = sb("qbuf", [P, NJ * CMAX])
        qC = qbuf[:, 0:NJ * TB].rearrange("p (c j n) -> p c j n", c=NC, j=NJ)
        qS = qbuf[:, NJ * TB:].rearrange("p (j n) -> p j n", j=NJ)
        kT = sb("kT", [P, CH + CMAX])
        vA = sb("vA", [P, NT, P])
        vB = sb("vB", [P, NT + 1, P])
        vS = sb("vS", [KEYS_S, P])
        kcT = sb("kcT", [P, CH])
        raw = sb("raw", [P, RAW, WIDTH])
        wH, wL = sb("wH", [P, SPLIT, WIDTH], F32R), sb("wL", [P, SPLIT, WIDTH], F32R)
        work = sb("work", [P, 3, CMAX])
        sq = sb("sq", [P, 2, XWMAX])
        acc = sb("acc", [P, CMAX])
        diag = sb("diag", [P, XWMAX])
        xb = sb("xb", [P, 3, XWMAX])
        carry = sb("carry", [P, G, 16])
        carry_s = sb("carry_s", [P, G, 16])
        state = sb("state", [P, G, 16])
        pr = sb("pr", [P, 2, 4 * P])
        prT = sb("prT", [P, 2, 4 * P])
        rope = sb("rope", [P, 2, CMAX])
        rms = sb("rms", [P, CMAX])
        cst = sb("cst", [P, 2 * P + G * 16])
        ident, rot = cst[:, 0:P], cst[:, P:2 * P]
        head_scale = cst[:, 2 * P:].rearrange("p (g c) -> p g c", g=G)
        ones = sb("ones", [P, P])
        vec = sb("vec", [P, 4 * KD + 6])
        g_mix, p_scale, g_mlp, g_fin = (vec[:, i * KD:(i + 1) * KD] for i in range(4))
        nsink = sb("nsink", [P, 6])
        small = sb("small", [P, 64])
        mask0, eps = small[:, 0:1], small[:, 1:2]
        std = small[:, 2:7]
        rstd = {"x": small[:, 40:45], "h": small[:, 7:12], "f": small[:, 7:12]}
        smax, negm, sinkd, esink, rsum, den, rden = (small[:, 12 + 4 * i:16 + 4 * i] for i in range(7))

        prod = [ctx.enter_context(nc.psum_tensor(f"prod{i}", [P, 2, 512], F32)) for i in range(2)]
        auxA = ctx.enter_context(nc.psum_tensor("auxA", [P, 2, 512], F32))
        auxB = ctx.enter_context(nc.psum_tensor("auxB", [P, 2, 512], F32))

        def pview(t, b):
            return t[:, 0:2, 0:CMAX // 2] if b == 0 else t[:, 0:1, 0:TB]

        def sview(ap, b):
            return ap[:, 0:cols(b)].rearrange("p (s n) -> p s n", s=2 if b == 0 else 1)

        def f(ap):
            return ap.bitcast(F32)

        raw_in = [sem(f"raw_in{i}") for i in range(RAW)]
        vec_in, const_in, x_in = sem("vec_in"), sem("const_in"), sem("x_in")
        rope_in, sample_in = sem("rope_in"), sem("sample_in")
        x_first = [sem(f"x_first{i}") for i in range(KD)]
        y_out = [sem(f"y_out{i}") for i in range(KD // 2)]
        kv_out, pool_out, copy_out = sem("kv_out"), sem("pool_out"), sem("copy_out")
        start = sem("start")
        w_high, w_low = sem("w_high"), sem("w_low")
        prod_done = sem("prod_done")
        relu_done, hid_sq = sem("relu_done"), sem("hid_sq")
        hid_high, hid_low = sem("hid_high"), sem("hid_low")
        down_added = sem("down_added")
        vec_chain, pool_chain = sem("vec_chain"), sem("pool_chain")

        norms = [("x", 0)]
        for b in range(NB):
            norms += [("h", b)] + ([("x", b + 1)] if b + 1 < NB else []) + [("f", b)]
        inner = [n for n in norms if n[0] != "f"]
        blocks = range(NB)
        s_sq = Signal("squared", [(*n, k) for n in norms for k in range(KD)])
        s_acc = Signal("squares_added", [(*n, k) for n in norms for k in range(1, KD)])
        s_stat = Signal("squares_summed", norms)
        s_std = Signal("root_taken", norms)
        s_rstd = Signal("root_inverted", norms)
        s_diag = Signal("rstd_on_diagonal", norms)
        s_bc = Signal("rstd_spread", norms)
        s_nH = Signal("gained_high", [(*n, k) for n in inner for k in range(KD)])
        s_nL = Signal("gained_low", [(*n, k) for n in inner for k in range(KD)])
        s_r = Signal("rms_kept", inner)
        s_tab = Signal("angles_scaled", [(b,) for b in blocks])
        s_y = Signal("y_normed", [(b, k) for b in blocks for k in range(KD)])
        s_tmp = Signal("qkv_copied", [(b, i) for b in blocks for i in range(6)])
        s_rot = Signal("halves_swapped", [(b, i) for b in blocks for i in range(5)])
        s_q = Signal("rotated", [(b, i) for b in blocks for i in range(5)])
        s_vt = Signal("v_transposed", [(b,) for b in blocks])
        s_vA = Signal("vA_copied", [(b,) for b in blocks])
        s_vB = Signal("vB_copied", [(b,) for b in blocks])
        groups = [(b, g) for b in blocks for g in range(G)]
        s_xb = Signal("pool_in_copied", groups)
        s_carry = Signal("pool_carried", groups)
        s_p = Signal("pooled", groups)
        s_pH = Signal("pooled_high", groups)
        s_pL = Signal("pooled_low", groups)
        chunks = [(b, c) for b in blocks for c in range(nchunks(b))]
        s_sc = Signal("scores", chunks)
        s_negm = Signal("max_negated", chunks)
        s_exp = Signal("exps", chunks)
        s_prn = Signal("probs_normed", chunks)
        s_pt = Signal("probs_transposed", chunks)
        s_ptS = Signal("probs_copied", chunks)
        s_pv = Signal("values_mixed", chunks)
        s_aH = Signal("attn_high", chunks)
        s_aL = Signal("attn_low", chunks)
        tiles = [(b, m) for b in blocks for m in range(KD)]
        s_gz = Signal("gate_scaled", [(b, kind, m) for b in blocks for kind in ("gp", "ga") for m in range(KD)])
        s_gp = Signal("pool_gate", tiles)
        s_pp = Signal("pool_up", tiles)
        s_pool = Signal("pool_gated", tiles)
        s_ga = Signal("attn_gate", tiles)
        s_gat = Signal("attn_gated", tiles)
        s_mrg = Signal("merged", tiles)
        s_mH = Signal("merged_high", tiles)
        s_mL = Signal("merged_low", tiles)
        s_h = Signal("h_added", tiles)

        def wait(eng, signal, *item):
            eng.wait_ge(signal.sem, signal.count[item])

        def unit_width(u):
            return AO_WIDTH if u < M_MLP and MIXER[u][0] == "ao" else WIDTH

        def wait_product(eng, b, i):
            eng.wait_ge(prod_done, b * UNITS + i + 1)

        def wait_mlp(eng, b, q, i):
            eng.wait_ge(prod_done, 16 * q + (b * UNITS + M_MLP + i + 1))

        def hid(b, q, m):
            return 8 * q + (b * KD * NQ + m + 1)

        def quarters(eng, b, up, down, last):
            up(b, 0)
            with eng.Fori(0, NQ - 1) as q:
                down(b, q)
                up(b, q + 1)
            last(b)

        block = ctx.enter_context(nc.Block())

        @block.sync
        def _(sp):
            def load_mixer_unit(b, u):
                n = b * UNITS + u
                if n >= RAW:
                    sp.wait_ge(w_low, n - RAW + 1)
                w = unit_width(u)
                sp.dma_start(raw[:, n % RAW, 0:w], weights[u, :, 0:w]).then_inc(raw_in[n % RAW], 16)

            def load_mlp_unit(b, q, i):
                sp.wait_ge(w_low, 16 * q + (b * UNITS + M_MLP + i - RAW + 1))
                slot = (b * UNITS + M_MLP + i) % RAW
                sp.dma_start(raw[:, slot, :], weights[16 * q + (M_MLP + i), :, :]).then_inc(raw_in[slot], 16)

            def load_rope(b):
                if b > 0:
                    wait(sp, s_q, b - 1, NJ)
                sp.dma_start(rope[:, :, 0:TB], tables[:, :, b * TB:(b + 1) * TB]).then_inc(rope_in, 16)
                if b == 0:
                    sp.dma_start(rope[:, :, TB:CMAX], tables[:, :, SEQ:SEQ + DEC]).then_inc(rope_in, 16)

            sp.dma_start(vec[:, :], vectors).then_inc(vec_in, 16)
            load_mixer_unit(0, 0)
            for k in range(KD):
                sp.dma_start(xT[:, k, :], x0[:, k, :]).then_inc(x_first[k], 16)
            load_mixer_unit(0, 1)
            sp.dma_start(cst[:, :], consts).then_inc(const_in, 16)
            load_mixer_unit(0, 2)
            load_rope(0)
            load_mixer_unit(0, 3)
            sp.dma_start(kcT[:, :], kcache_t).then_inc(sample_in, 16)
            sp.dma_start(vS[DEC:KEYS_S, :], vcache).then_inc(sample_in, 16)
            sp.dma_start(state[:, :, :], state_s).then_inc(sample_in, 16)
            sp.dma_start(k_old_out, kold).then_inc(copy_out, 16)
            sp.dma_start(v_old_out, vold).then_inc(copy_out, 16)

            def up(b, q):
                for m in range(KD):
                    load_mlp_unit(b, q, m)
                    if isinstance(q, int) and m == 3 and b + 1 < NB:
                        wait(sp, s_h, b, KD - 1)
                        sp.dma_start(xT[:, :, 0:TB], x123[b, :, :, :]).then_inc(x_in, 16)

            def down(b, q):
                for m in range(KD):
                    load_mlp_unit(b, q, KD + m)

            for b in blocks:
                for u in range(RAW if b == 0 else 0, M_MLP):
                    load_mixer_unit(b, u)
                    if u == ROPE_LOAD and b + 1 < NB:
                        load_rope(b + 1)
                quarters(sp, b, up, down, lambda b: down(b, NQ - 1))
            sp.wait_ge(copy_out, 32)

        @block.tensor
        def _(pe):
            def stream(out, b, lhs, rhs, first, last):
                for s, lo, hi in ((0, 0, 272), (1, 272, CMAX)) if b == 0 else ((0, 0, TB),):
                    ins = nc.tensor.matmul(out[:, s, 0:hi - lo], lhs, rhs[:, lo:hi], start=first, stop=last)
                return ins

            def three(out, b, uslot, off, high, low, k, first, last):
                wh, wl = wH[:, uslot, off:off + P], wL[:, uslot, off:off + P]
                stream(out, b, wh, high[:, k, :], first, False)
                stream(out, b, wh, low[:, k, :], False, False)
                return stream(out, b, wl, high[:, k, :], False, last)

            def product(b, slot, high, low, nk, before_k=None):
                for k in range(nk):
                    if before_k:
                        before_k(k)
                    ins = three(prod[slot], b, slot, k * P, high, low, k, k == 0, k == nk - 1)
                ins.then_inc(prod_done, 1)

            def wait_read(b, i):
                if i < 2:
                    if b > 0:
                        pe.wait_ge(down_added, hid(b - 1, NQ - 1, KD - 2 + i))
                    return
                kind, m = MIXER[i - 2]
                signal = {"qkv": s_tmp, "xp": s_xb, "gp": s_gz, "ga": s_gz, "ao": s_gat, "out": s_h}[kind]
                wait(pe, signal, b, *((kind, m) if signal is s_gz else (m,)))

            def mixer_product(b, i):
                kind, m = MIXER[i]
                pe.wait_ge(w_low, b * UNITS + i + 1)
                high, low, nk = {"ao": (attH, attL, NJ), "out": (midH, midL, KD)}.get(kind, (nH, nL, KD))
                if kind == "ao":
                    if m == 0:
                        wait(pe, s_aL, b, nchunks(b) - 1)
                    else:
                        wait(pe, s_pool, b, m - 1)
                    g = m // 2
                    wait(pe, s_pL, b, g)
                    three(auxB, b, i % 2, NJ * P, midH, midL, POOLED + g, True, True).then_inc(s_pp.sem, 1)
                wait_read(b, i)

                def before(k):
                    if i == 0:
                        wait(pe, s_nL, "x", b, k)
                    if kind == "out" and m == 0:
                        wait(pe, s_mL, b, k)
                    if (b, i, k) == (0, 1, 5):
                        sum_squares("x", 0)
                    if (b, i, k) == (0, 2, 2):
                        spread("x", 0)
                product(b, i % 2, high, low, nk, before)

            def sum_squares(kind, b):
                wait(pe, s_acc, kind, b, KD - 1)
                if (kind, b) == ("x", 0):
                    pe.wait_ge(start, 1)
                if kind == "f" and b + 1 < NB:
                    wait(pe, s_r, "x", b + 1)
                for t in range(NT):
                    ins = nc.tensor.matmul(auxA[:, 1, t:t + 1], acc[:, t * P:(t + 1) * P], ones[:, 0:1],
                                           start=True, stop=True)
                if b == 0:
                    ins = nc.tensor.matmul(auxA[0:DEC, 1, NT:NT + 1], acc[:, TB:CMAX], ones[:, 0:1],
                                           start=True, stop=True)
                ins.then_inc(s_stat.sem, 1)

            def spread(kind, b):
                wait(pe, s_diag, kind, b)
                if b == 0:
                    nc.tensor.matmul(auxA[:, 0, 0:272], ones[:, :], diag[:, 0:272], start=True, stop=True)
                    nc.tensor.matmul(auxA[:, 1, 0:240], ones[:, :], diag[:, 272:TB], start=True, stop=True)
                    ins = nc.tensor.matmul(auxA[:, 1, 240:272], ones[0:DEC, :], diag[0:DEC, TB:CMAX],
                                           start=True, stop=True)
                else:
                    ins = nc.tensor.matmul(auxA[:, 0, :], ones[:, :], diag[:, 0:TB], start=True, stop=True)
                ins.then_inc(s_bc.sem, 1)

            def swap_halves(b, i):
                wait(pe, s_tmp, b, i)
                if b == 0:
                    pe.wait_ge(const_in, 16)
                if i > 0:
                    wait(pe, s_q, b, i - 1)
                stream(auxB, b, rot, work[:, i % 2, :], True, True).then_inc(s_rot.sem, 1)

            def transpose_v(b):
                wait(pe, s_tmp, b, 5)
                if b > 0:
                    wait(pe, s_y, b - 1, KD - 1)
                for t in range(NT):
                    ins = nc.tensor.transpose(auxA[:, 1, t * P:(t + 1) * P], work[:, 1, t * P:(t + 1) * P], ident)
                if b == 0:
                    ins = nc.tensor.transpose(auxA[0:DEC, 0, 0:P], work[:, 1, TB:CMAX], ident)
                ins.then_inc(s_vt.sem, 1)

            def scores(b, c):
                if c >= 1:
                    wait(pe, s_exp, b, c - 1)
                else:
                    wait(pe, s_q, b, 4)
                    wait(pe, s_vA, b)
                if c == NC:
                    pe.wait_ge(sample_in, 48)
                for g in range(KV):
                    rows, bank = slice(g * HD, (g + 1) * HD), auxA[:, g, :]
                    if c == NC:
                        q = qbuf[rows, NJ * TB:]
                        nc.tensor.matmul(bank[:, 0:DEC], q, kT[rows, CH + TB:CH + CMAX],
                                         start=True, stop=True)
                        ins = nc.tensor.matmul(bank[:, DEC:KEYS_S], q, kcT[rows, :],
                                               start=True, stop=True)
                        continue
                    for pair in range(2):
                        at = pair * P
                        q = qbuf[rows, (4 * c + 2 * pair) * CH:(4 * c + 2 * pair + 2) * CH]
                        if c % 2:
                            ins = nc.tensor.matmul(bank[:, at:at + P], q, kT[rows, c * CH:(c + 2) * CH],
                                                   start=True, stop=True)
                        else:
                            nc.tensor.matmul(bank[:, at:at + CH], q, kT[rows, (c + 1) * CH:(c + 2) * CH],
                                             start=True, stop=True)
                            ins = nc.tensor.matmul(bank[:, at + CH:at + P], q, kT[rows, c * CH:(c + 1) * CH],
                                                   start=True, stop=True)
                ins.then_inc(s_sc.sem, 1)

            def transpose_probs(b, c):
                wait(pe, s_prn, b, c)
                if c >= 1:
                    wait(pe, s_ptS, b, c - 1)
                if c == NC:
                    for g in range(KV):
                        ins = nc.tensor.transpose(auxB[0:KEYS_S, 1, g * P:(g + 1) * P],
                                                  pr[:, 0, g * KEYS_S:(g + 1) * KEYS_S], ident)
                else:
                    for i in range(4):
                        ins = nc.tensor.transpose(auxB[:, 1, i * P:(i + 1) * P], pr[:, c % 2, i * P:(i + 1) * P], ident)
                ins.then_inc(s_pt.sem, 1)

            def mix_values(b, c):
                wait(pe, s_ptS, b, c)
                if c >= 1:
                    wait(pe, s_aL, b, c - 1)
                else:
                    wait(pe, s_vB, b)
                for g in range(KV):
                    feats = slice(g * HD, (g + 1) * HD)
                    if c == NC:
                        ins = nc.tensor.matmul(auxB[feats, 0, 0:P], vS[:, feats], prT[0:KEYS_S, 0, g * P:(g + 1) * P],
                                               start=True, stop=True)
                    else:
                        v = vA if c % 2 else vB
                        ins = nc.tensor.matmul(auxB[feats, 0, 0:2 * P], v[:, c // 2, feats],
                                               prT[:, c % 2, 2 * g * P:2 * (g + 1) * P], start=True, stop=True)
                ins.then_inc(s_pv.sem, 1)

            def between(b, i):
                if b > 0 and i == 0:
                    sum_squares("f", b - 1)
                if b > 0 and i == 1:
                    spread("f", b - 1)
                if 1 <= i <= 5:
                    swap_halves(b, i - 1)
                if i == 6:
                    transpose_v(b)
                if 0 <= i - ATT0 - 2 < nchunks(b):
                    mix_values(b, i - ATT0 - 2)
                if 0 <= i - ATT0 - 1 < nchunks(b):
                    transpose_probs(b, i - ATT0 - 1)
                if 0 <= i - ATT0 < nchunks(b):
                    scores(b, i - ATT0)

            def up(b, q):
                for m in range(KD):
                    first = isinstance(q, int) and q == 0
                    if m >= 2:
                        pe.wait_ge(relu_done, hid(b, q, m - 2))
                    elif first:
                        wait(pe, s_h, b, KD - 2 + m)
                    else:
                        pe.wait_ge(down_added, hid(b, q - 1, KD - 2 + m))
                    pe.wait_ge(w_low, 16 * q + (b * UNITS + M_MLP + m + 1))

                    def before(k):
                        if first and m == 0:
                            wait(pe, s_nL, "h", b, k)
                        if first and (m, k) == (0, 6):
                            sum_squares("h", b)
                        if first and (m, k) == (1, 2):
                            spread("h", b)
                    product(b, m % 2, nH, nL, KD, before)

            def down(b, q):
                for m in range(KD):
                    if m >= 2:
                        pe.wait_ge(down_added, hid(b, q, m - 2))
                    else:
                        pe.wait_ge(relu_done, hid(b, q, KD - 2 + m))
                    pe.wait_ge(w_low, 16 * q + (b * UNITS + M_MLP + KD + m + 1))
                    before = (lambda k: pe.wait_ge(hid_low, hid(b, q, k))) if m == 0 else None
                    product(b, m % 2, midH, midL, KD, before)
                    if isinstance(q, int) and q == NQ - 1 and b + 1 < NB:
                        if m == 0:
                            sum_squares("x", b + 1)
                        if m == 1:
                            spread("x", b + 1)

            for b in blocks:
                for i in range(M_MLP):
                    mixer_product(b, i)
                    between(b, i)
                quarters(pe, b, up, down, lambda b: down(b, NQ - 1))
            sum_squares("f", NB - 1)
            spread("f", NB - 1)

        @block.scalar
        def _(act):
            def copy(out, in_, scale=1.0):
                return nc.scalar.activation(out, in_, ACT.Copy, scale=scale)

            def split_high(b, u):
                n = b * UNITS + u
                if n >= NB * UNITS:
                    return
                w = unit_width(u % UNITS)
                act.wait_ge(raw_in[n % RAW], 16 * (n // RAW + 1))
                copy(wH[:, n % 2, 0:w], raw[:, n % RAW, 0:w]).then_inc(w_high, 1)

            def split_high_mlp(b, q, i):
                n = b * UNITS + M_MLP + i
                act.wait_ge(raw_in[n % RAW], 64 * q + 16 * (n // RAW + 1))
                copy(wH[:, n % 2, :], raw[:, n % RAW, :]).then_inc(w_high, 1)

            def square(kind, b, k, src):
                at = norms.index((kind, b))
                if k >= 2:
                    wait(act, s_acc, kind, b, max(1, k - 2))
                elif at:
                    wait(act, s_acc, *norms[at - 1], KD - 1)
                nc.scalar.activation(sview(sq[:, k % 2, :], b), sview(src[:, k, :], b), ACT.Square).then_inc(s_sq.sem, 1)

            def root(kind, b):
                wait(act, s_stat, kind, b)
                ins = nc.scalar.activation(std[:, 0:NT], auxA[:, 1, 0:NT], ACT.Sqrt, bias=eps, scale=1.0 / D)
                if b == 0:
                    ins = nc.scalar.activation(std[0:DEC, NT:NT + 1], auxA[0:DEC, 1, NT:NT + 1], ACT.Sqrt,
                                               bias=eps[0:DEC], scale=1.0 / D)
                ins.then_inc(s_std.sem, 1)

            def gained_high(kind, b, k):
                src, gain = (xT, g_mix) if kind == "x" else (hT, g_mlp)
                copy(nH[:, k, 0:cols(b)], src[:, k, 0:cols(b)], gain[:, k:k + 1]).then_inc(s_nH.sem, 1)

            def keep_rms(kind, b):
                wait(act, s_bc, kind, b)
                copy(sview(rms, b), pview(auxA, b)).then_inc(s_r.sem, 1)

            def exps(b, c):
                wait(act, s_negm, b, c)
                n, w = (KV, KEYS_S) if c == NC else (4, P)
                for i in range(n):
                    at = i % (n // KV) * w
                    nc.scalar.activation(pr[:, c % 2, i * w:(i + 1) * w], auxA[:, i * KV // n, at:at + w], ACT.Exp,
                                         bias=negm[:, i:i + 1], scale=SCALE, accum_out=rsum[:, i:i + 1])
                nc.scalar.activation(esink[:, 0:n], sinkd[:, 0:n], ACT.Exp).then_inc(s_exp.sem, 1)

            def copy_probs(b, c):
                wait(act, s_pt, b, c)
                if c == NC:
                    copy(prT[0:KEYS_S, 0, 0:2 * P], auxB[0:KEYS_S, 1, 0:2 * P]).then_inc(s_ptS.sem, 1)
                else:
                    copy(prT[:, c % 2, :], auxB[:, 1, :]).then_inc(s_ptS.sem, 1)

            def attn_high(b, c):
                wait(act, s_pv, b, c)
                w = DEC if c == NC else CH
                copy(attH[:, :, c * CH:c * CH + w],
                     auxB[:, 0, 0:NJ * w].rearrange("p (j n) -> p j n", j=NJ)).then_inc(s_aH.sem, 1)

            def merged_high(b, m):
                wait(act, s_mrg, b, m)
                copy(midH[:, m, 0:cols(b)], hT[:, m, 0:cols(b)], 0.5).then_inc(s_mH.sem, 1)

            def pooled_high(b, g):
                wait(act, s_p, b, g)
                ins = copy(midH[:, POOLED + g, 0:TB], diag[:, 16:XW])
                if b == 0:
                    ins = copy(midH[:, POOLED + g, TB:CMAX], diag[:, XWMAX - DEC:XWMAX])
                ins.then_inc(s_pH.sem, 1)

            def store_y(b, part):
                wait(act, s_y, b, 2 * part + 1)
                ks = slice(2 * part, 2 * part + 2)
                dst = y0[:, ks, :] if b == 0 else y123[b - 1, :, ks, :]
                act.dma_start(dst, hT[:, ks, 0:cols(b)]).then_inc(y_out[part], 16)

            def step(b, i):
                kind, m = MIXER[i]
                wait_product(act, b, i)
                if kind == "qkv":
                    if m >= 2:
                        wait(act, s_q, b, m - 2)
                    copy(sview(work[:, m % 2, :], b), pview(prod[i % 2], b)).then_inc(s_tmp.sem, 1)
                split_high(b, i + 2)
                if kind == "gp":
                    wait(act, s_gz, b, "gp", m)
                    gate = hT[:, m, 0:cols(b)]
                    nc.scalar.activation(gate, gate, ACT.Tanh, scale=0.5).then_inc(s_gp.sem, 1)
                if kind == "ga":
                    wait(act, s_gz, b, "ga", m)
                    gate = work[:, m % 2, 0:cols(b)]
                    nc.scalar.activation(gate, gate, ACT.Tanh, scale=0.5).then_inc(s_ga.sem, 1)
                if kind == "ao":
                    merged_high(b, m)
                if kind == "out":
                    wait(act, s_h, b, m)
                    gained_high("h", b, m)
                    square("h", b, m, hT)
                if (b, i) == (0, 0):
                    root("x", 0)
                if (b, i) == (0, 1):
                    keep_rms("x", 0)
                if b > 0 and i == 0:
                    root("f", b - 1)
                if b > 0 and 2 <= i <= 5:
                    store_y(b - 1, i - 2)
                if i == 6:
                    wait(act, s_vt, b)
                    if b == 0:
                        copy(vS[0:DEC, :], auxA[0:DEC, 0, 0:P], rstd["x"][0:DEC, NT:NT + 1])
                    for t in range(NT):
                        ins = copy(vA[:, t, :], auxA[:, 1, t * P:(t + 1) * P], rstd["x"][:, t:t + 1])
                    ins.then_inc(s_vA.sem, 1)
                    if b in (0, NB - 1):
                        wait(act, s_q, b, NJ)
                        wait(act, s_vA, b)
                    if b == 0:
                        act.dma_start(ks_new, kT[:, CH + TB:CH + CMAX]).then_inc(kv_out, 16)
                        act.dma_start(vs_new, vS[0:DEC, :]).then_inc(kv_out, 16)
                    if b == NB - 1:
                        act.dma_start(k_new, kT[:, CH + TB - P:CH + TB]).then_inc(kv_out, 16)
                        act.dma_start(v_new, vA[:, NT - 1, :]).then_inc(kv_out, 16)
                if 0 <= i - ATT0 - 2 < nchunks(b):
                    attn_high(b, i - ATT0 - 2)
                if 0 <= i - ATT0 - 1 < nchunks(b):
                    copy_probs(b, i - ATT0 - 1)
                if 0 <= i - ATT0 < nchunks(b):
                    exps(b, i - ATT0)
                if i in (8, 10, 12, 15):
                    pooled_high(b, (8, 10, 12, 15).index(i))
                if i == 20 and b in (0, NB - 1):
                    wait(act, s_carry, b, G - 1)
                    if b == 0:
                        act.dma_start(ps_new, carry_s[:, :, :]).then_inc(pool_out, 16)
                    else:
                        act.dma_start(p_new, carry[:, :, :]).then_inc(pool_out, 16)

            def up(b, q):
                first = isinstance(q, int) and q == 0
                for m in range(KD):
                    wait_mlp(act, b, q, m)
                    split_high_mlp(b, q, m + 2)
                    if first and m == 0:
                        keep_rms("h", b)
                    act.wait_ge(relu_done, hid(b, q, m))
                    nc.scalar.activation(midH[:, m, 0:cols(b)], work[:, m % 2, 0:cols(b)], ACT.Square).then_inc(hid_high, 1)
                    if first and b + 1 < NB and m >= 4:
                        if m == 4:
                            act.wait_ge(x_in, 16 * (b + 1))
                        square("x", b + 1, 2 * m - 8, xT)
                        square("x", b + 1, 2 * m - 7, xT)

            def down(b, q):
                for m in range(KD):
                    wait_mlp(act, b, q, KD + m)
                    split_high_mlp(b, q, KD + m + 2)

            def last_down(b):
                for m in range(KD):
                    wait_mlp(act, b, NQ - 1, KD + m)
                    split_high(b, UNITS - KD + m + 2)
                    act.wait_ge(down_added, hid(b, NQ - 1, m))
                    square("f", b, m, hT)
                    if b + 1 < NB:
                        gained_high("x", b + 1, m)
                        if m == 0:
                            root("x", b + 1)
                        if m == 2:
                            keep_rms("x", b + 1)

            split_high(0, 0)
            act.wait_ge(vec_in, 16)
            for k in range(KD):
                act.wait_ge(x_first[k], 16)
                gained_high("x", 0, k)
            split_high(0, 1)
            for k in range(KD):
                square("x", 0, k, xT)
            act.wait_ge(start, 1)
            for b in blocks:
                for i in range(M_MLP):
                    step(b, i)
                root("h", b)
                quarters(act, b, up, down, last_down)
            root("f", NB - 1)
            for part in range(KD // 2):
                store_y(NB - 1, part)
            for part in range(KD // 2):
                act.wait_ge(y_out[part], 16 * NB)
            act.wait_ge(kv_out, 64)
            act.wait_ge(pool_out, 32)

        @block.vector
        def _(dve):
            tt, stt = nc.vector.tensor_tensor, nc.vector.scalar_tensor_tensor
            chain = [0]

            def link(ins):
                chain[0] += 1
                ins.then_inc(vec_chain, 1)
                dve.wait_ge(vec_chain, chain[0])

            def low(out, x, high):
                return tt(out, x, f(high), ALU.subtract)

            def split_low(b, u):
                n = b * UNITS + u
                if n >= NB * UNITS:
                    return
                w = unit_width(u % UNITS)
                dve.wait_ge(w_high, n + 1)
                low(wL[:, n % 2, 0:w], raw[:, n % RAW, 0:w], wH[:, n % 2, 0:w]).then_inc(w_low, 1)

            def split_low_mlp(b, q, i):
                n = b * UNITS + M_MLP + i
                dve.wait_ge(w_high, 16 * q + (n + 1))
                low(wL[:, n % 2, :], raw[:, n % RAW, :], wH[:, n % 2, :]).then_inc(w_low, 1)

            def add_square(kind, b, k):
                wait(dve, s_sq, kind, b, k)
                n = cols(b)
                if k == 1:
                    tt(acc[:, 0:n], sq[:, 0, 0:n], sq[:, 1, 0:n], ALU.add).then_inc(s_acc.sem, 1)
                elif k > 1:
                    wait(dve, s_acc, kind, b, k - 1)
                    tt(acc[:, 0:n], acc[:, 0:n], sq[:, k % 2, 0:n], ALU.add).then_inc(s_acc.sem, 1)

            def invert(kind, b):
                wait(dve, s_std, kind, b)
                r = rstd[kind]
                ins = nc.vector.reciprocal(r[:, 0:NT], std[:, 0:NT])
                if b == 0:
                    ins = nc.vector.reciprocal(r[0:DEC, NT:NT + 1], std[0:DEC, NT:NT + 1])
                ins.then_inc(s_rstd.sem, 1)
                wait(dve, s_rstd, kind, b)
                ins = tt(diag[:, 0:TB].rearrange("p (t n) -> p t n", t=NT),
                         ident.unsqueeze(1).to_broadcast([P, NT, P]),
                         r[:, 0:NT].unsqueeze(2).to_broadcast([P, NT, P]), ALU.mult)
                if b == 0:
                    ins = tt(diag[0:DEC, TB:CMAX], ident[0:DEC, 0:DEC],
                             r[0:DEC, NT:NT + 1].to_broadcast([DEC, DEC]), ALU.mult)
                ins.then_inc(s_diag.sem, 1)

            def gained_low(kind, b, k):
                src, gain = (xT, g_mix) if kind == "x" else (hT, g_mlp)
                wait(dve, s_nH, kind, b, k)
                n = cols(b)
                stt(out=nL[:, k, 0:n], in0=src[:, k, 0:n], scalar=gain[:, k:k + 1], in1=f(nH[:, k, 0:n]),
                    op0=ALU.mult, op1=ALU.subtract).then_inc(s_nL.sem, 1)

            def scale_angles(b):
                dve.wait_ge(rope_in, 16 * (b + 2))
                wait(dve, s_r, "x", b)
                table = rope[:, :, 0:cols(b)]
                tt(table, table, rms[:, 0:cols(b)].unsqueeze(1).to_broadcast([P, 2, cols(b)]),
                   ALU.mult).then_inc(s_tab.sem, 1)

            def final(b, k):
                if k == 0:
                    wait(dve, s_bc, "f", b)
                stt(out=sview(hT[:, k, :], b), in0=sview(hT[:, k, :], b), scalar=g_fin[:, k:k + 1],
                    in1=pview(auxA, b), op0=ALU.mult, op1=ALU.mult).then_inc(s_y.sem, 1)

            def rotate(b, i):
                n = cols(b)
                q = work[:, i % 2, :]
                wait(dve, s_tab, b)
                wait(dve, s_rot, b, i)
                tt(sview(work[:, 2, :], b), pview(auxB, b), sview(rope[:, 1, :], b), ALU.mult)
                link(tt(q[:, 0:n], q[:, 0:n], rope[:, 0, 0:n], ALU.mult))
                if i == NJ:
                    ins = tt(kT[:, CH:CH + n], q[:, 0:n], work[:, 2, 0:n], ALU.add)
                else:
                    by_chunk = lambda ap: ap[:, 0:TB].rearrange("p (c n) -> p c n", c=NC)
                    ins = tt(qC[:, :, i, :], by_chunk(q), by_chunk(work[:, 2, :]), ALU.add)
                    if b == 0:
                        ins = tt(qS[:, i, :], q[:, TB:CMAX], work[:, 2, TB:CMAX], ALU.add)
                ins.then_inc(s_q.sem, 1)
                wait(dve, s_q, b, i)

            def row_max(b, c):
                wait(dve, s_sc, b, c)
                n, w = (KV, KEYS_S) if c == NC else (4, P)
                sc = auxA[:, :, 0:n // KV * w].rearrange("p g (i k) -> p g i k", k=w)
                sink = nsink[:, 4:6] if c == NC else nsink[:, 0:4]
                if b == 0 and c == 0:
                    link(nc.vector.tensor_scalar(sc[:, :, :, CH:P], sc[:, :, :, CH:P], MASKED, None, ALU.add))
                link(nc.vector.tensor_reduce(smax[:, 0:n].rearrange("p (g i) -> p g i", g=KV), sc, AX, ALU.max))
                link(stt(out=negm[:, 0:n], in0=smax[:, 0:n], scalar=-SCALE, in1=sink, op0=ALU.mult, op1=ALU.min))
                tt(sinkd[:, 0:n], negm[:, 0:n], sink, ALU.subtract).then_inc(s_negm.sem, 1)

            def norm_probs(b, c):
                wait(dve, s_exp, b, c)
                n, w = (KV, KEYS_S) if c == NC else (4, P)
                link(tt(den[:, 0:n], rsum[:, 0:n], esink[:, 0:n], ALU.add))
                link(nc.vector.reciprocal(rden[:, 0:n], den[:, 0:n]))
                p = pr[:, c % 2, 0:n * w].rearrange("p (i k) -> p i k", i=n)
                tt(p, p, rden[:, 0:n].unsqueeze(2).to_broadcast([P, n, w]), ALU.mult).then_inc(s_prn.sem, 1)

            def attn_low(b, c):
                wait(dve, s_aH, b, c)
                w = DEC if c == NC else CH
                at = slice(c * CH, c * CH + w)
                low(attL[:, :, at], auxB[:, 0, 0:NJ * w].rearrange("p (j n) -> p j n", j=NJ),
                    attH[:, :, at]).then_inc(s_aL.sem, 1)

            def xp_out(b, m):
                if m == 3:
                    wait(dve, s_p, b, 0)
                elif b > 0:
                    wait(dve, s_p, b - 1, 3 if m == 0 else m)
                src, to = pview(prod[m % 2], b), xb[:, m % 3, :]
                if b == 0:
                    tt(to[:, 16:16 + 272], src[:, 0, :], rms[:, 0:272], ALU.mult)
                    tt(to[:, 16 + 272:XW], src[:, 1, 0:240], rms[:, 272:TB], ALU.mult)
                    ins = tt(to[:, XWMAX - DEC:XWMAX], src[:, 1, 240:272], rms[:, TB:CMAX], ALU.mult)
                else:
                    ins = tt(to[:, 16:XW], src[:, 0, :], rms[:, 0:TB], ALU.mult)
                ins.then_inc(s_xb.sem, 1)

            def scale_gate(b, kind, m, to):
                tt(sview(to, b), pview(prod[m % 2 if kind == "gp" else 0], b), sview(rms, b),
                   ALU.mult).then_inc(s_gz.sem, 1)

            def gate_pool(b, m):
                wait(dve, s_pp, b, m)
                wait(dve, s_gp, b, m)
                h = sview(hT[:, m, :], b)
                stt(out=h, in0=h, scalar=1.0, in1=pview(auxB, b), op0=ALU.add, op1=ALU.mult).then_inc(s_pool.sem, 1)

            def merge(b, i, m):
                n = cols(b)
                wait(dve, s_ga, b, m)
                t = work[:, m % 2, :]
                stt(out=sview(t, b), in0=sview(t, b), scalar=1.0, in1=pview(prod[i % 2], b),
                    op0=ALU.add, op1=ALU.mult).then_inc(s_gat.sem, 1)
                wait(dve, s_gat, b, m)
                wait(dve, s_pool, b, m)
                stt(out=hT[:, m, 0:n], in0=hT[:, m, 0:n], scalar=p_scale[:, m:m + 1], in1=t[:, 0:n],
                    op0=ALU.mult, op1=ALU.add).then_inc(s_mrg.sem, 1)

            def step(b, i):
                kind, m = MIXER[i]
                n = cols(b)
                if kind == "ao":
                    gate_pool(b, m)
                wait_product(dve, b, i)
                if kind == "xp":
                    xp_out(b, m)
                if kind == "gp":
                    if b > 0:
                        dve.wait_ge(y_out[m // 2], 16 * b)
                    scale_gate(b, kind, m, hT[:, m, :])
                if kind == "ga":
                    scale_gate(b, kind, m, work[:, m % 2, :])
                if kind == "ao":
                    merge(b, i, m)
                if kind == "out":
                    tt(sview(hT[:, m, :], b), sview(xT[:, m, :], b), pview(prod[i % 2], b), ALU.add).then_inc(s_h.sem, 1)
                if b > 0 and i == 0:
                    link(nc.vector.tensor_copy(kT[:, 0:CH], kT[:, TB:TB + CH]))
                    add_square("f", b - 1, KD - 1)
                    invert("f", b - 1)
                if i == 6:
                    wait(dve, s_vA, b)
                    if b > 0:
                        link(nc.vector.tensor_copy(vB[CH:P, 0, :], vB[CH:P, NT, :]))
                    nc.vector.tensor_copy(vB[0:CH, 0:NT, :], vA[0:CH, :, :])
                    nc.vector.tensor_copy(vB[CH:P, 1:NT + 1, :], vA[CH:P, :, :]).then_inc(s_vB.sem, 1)
                if 0 <= i - ATT0 - 2 < nchunks(b):
                    attn_low(b, i - ATT0 - 2)
                if 0 <= i - ATT0 < nchunks(b):
                    row_max(b, i - ATT0)
                split_low(b, i + 2)
                if kind == "out":
                    gained_low("h", b, m)
                    add_square("h", b, m)
                if kind == "ao":
                    wait(dve, s_mH, b, m)
                    stt(out=midL[:, m, 0:n], in0=hT[:, m, 0:n], scalar=0.5, in1=f(midH[:, m, 0:n]),
                        op0=ALU.mult, op1=ALU.subtract).then_inc(s_mL.sem, 1)
                if (b, i) == (0, 0):
                    invert("x", 0)
                if (b, i) == (0, 1):
                    scale_angles(0)
                if 1 <= i <= 5:
                    rotate(b, i - 1)
                if b > 0 and 1 <= i <= 4:
                    final(b - 1, 2 * i - 2)
                    final(b - 1, 2 * i - 1)
                if 0 <= i - ATT0 < nchunks(b):
                    norm_probs(b, i - ATT0)

            def up(b, q):
                first = isinstance(q, int) and q == 0
                n = cols(b)
                for m in range(KD):
                    wait_mlp(dve, b, q, m)
                    if first and m == 0:
                        wait(dve, s_r, "h", b)
                    stt(out=sview(work[:, m % 2, :], b), in0=pview(prod[m % 2], b), scalar=0.0, in1=sview(rms, b),
                        op0=ALU.max, op1=ALU.mult).then_inc(relu_done, 1)
                    dve.wait_ge(relu_done, hid(b, q, m))
                    if m > 0 or not (first and b == 0):
                        dve.wait_ge(hid_low, hid(b, q, m - 1))
                    tt(work[:, 2, 0:n], work[:, m % 2, 0:n], work[:, m % 2, 0:n], ALU.mult).then_inc(hid_sq, 1)
                    split_low_mlp(b, q, m + 2)
                    dve.wait_ge(hid_high, hid(b, q, m))
                    dve.wait_ge(hid_sq, hid(b, q, m))
                    low(midL[:, m, 0:n], work[:, 2, 0:n], midH[:, m, 0:n]).then_inc(hid_low, 1)
                    if first and b + 1 < NB and m >= 4:
                        add_square("x", b + 1, 2 * m - 8)
                        add_square("x", b + 1, 2 * m - 7)

            def add_down(b, q, m):
                wait_mlp(dve, b, q, KD + m)
                tt(sview(hT[:, m, :], b), sview(hT[:, m, :], b), pview(prod[m % 2], b), ALU.add).then_inc(down_added, 1)

            def down(b, q):
                for m in range(KD):
                    add_down(b, q, m)
                    split_low_mlp(b, q, KD + m + 2)

            def last_down(b):
                for m in range(KD):
                    add_down(b, NQ - 1, m)
                    split_low(b, UNITS - KD + m + 2)
                    if m >= 2:
                        add_square("f", b, m - 1)
                    if b + 1 < NB:
                        gained_low("x", b + 1, m)
                        if m == 0:
                            invert("x", b + 1)
                        if m == 3:
                            scale_angles(b + 1)

            split_low(0, 0)
            for k in range(KD):
                gained_low("x", 0, k)
            split_low(0, 1)
            for k in range(KD):
                add_square("x", 0, k)
            dve.wait_ge(const_in, 16)
            dve.wait_ge(start, 1)
            nc.vector.tensor_scalar(nsink[:, :], vec[:, 4 * KD:4 * KD + 6], -1.0, None, ALU.mult)
            for b in blocks:
                for i in range(M_MLP):
                    step(b, i)
                invert("h", b)
                quarters(dve, b, up, down, last_down)
            add_square("f", NB - 1, KD - 1)
            invert("f", NB - 1)
            for k in range(KD):
                final(NB - 1, k)

        @block.gpsimd
        def _(pool):
            tt = nc.gpsimd.tensor_tensor

            def link(ins):
                chain[0] += 1
                ins.then_inc(pool_chain, 1)
                pool.wait_ge(pool_chain, chain[0])

            chain = [0]
            link(nc.gpsimd.memset(ones[:, :], 1.0))
            link(nc.gpsimd.memset(eps, EPS))
            link(nc.gpsimd.memset(kT[:, 0:CH], 0.0))
            nc.gpsimd.memset(vB[CH:P, 0, :], 0.0).then_inc(start, 1)
            pool.wait_ge(start, 1)
            pool.wait_ge(const_in, 16)
            pool.wait_ge(sample_in, 48)
            for b in blocks:
                w = XWMAX if b == 0 else XW
                if b > 0:
                    wait(pool, s_acc, "f", b - 1, KD - 1)
                    wait(pool, s_bc, "f", b - 1)
                for g in range(G):
                    x = xb[:, g % 3, :]
                    wait(pool, s_xb, b, g)
                    if b > 0:
                        wait(pool, s_carry, b - 1, g)
                    link(nc.gpsimd.tensor_copy(x[:, 0:16], carry[:, g, :]) if b > 0 else nc.gpsimd.memset(x[:, 0:16], 0.0))
                    if b == 0:
                        link(nc.gpsimd.tensor_copy(x[:, XW:XW + 16], state[:, g, :]))
                        link(nc.gpsimd.tensor_copy(carry_s[:, g, :], x[:, XWMAX - 16:XWMAX]))
                    nc.gpsimd.tensor_copy(carry[:, g, :], x[:, XW - 16:XW]).then_inc(s_carry.sem, 1)
                    src = x
                    for s in range(g + 1):
                        lo, dst = 2 ** (s + 1) - 1, sq[:, s % 2, :]
                        link(tt(dst[:, lo:w], src[:, lo:w], src[:, lo - 2 ** s:w - 2 ** s], ALU.add))
                        src = dst
                    link(nc.gpsimd.tensor_scalar(diag[:, 16:w], src[:, 16:w], 1.0 / 2 ** (g + 1), None, ALU.mult))
                    if b == 0:
                        link(tt(diag[:, 16:32], src[:, 16:32], head_scale[:, g, :], ALU.mult))
                    tt(diag[:, 16:w], diag[:, 16:w], x[:, 16:w], ALU.subtract).then_inc(s_p.sem, 1)
                    wait(pool, s_pH, b, g)
                    ins = tt(midL[:, POOLED + g, 0:TB], diag[:, 16:XW], f(midH[:, POOLED + g, 0:TB]), ALU.subtract)
                    if b == 0:
                        ins = tt(midL[:, POOLED + g, TB:CMAX], diag[:, XWMAX - DEC:XWMAX], f(midH[:, POOLED + g, TB:CMAX]), ALU.subtract)
                    ins.then_inc(s_pL.sem, 1)


def constants():
    eye = np.eye(P, dtype=np.float32)
    rot = np.zeros((P, P), np.float32)
    half = HD // 8
    for head in range(0, P, HD):
        for i in range(half):
            rot[head + half + i, head + i] = -1.0
            rot[head + i, head + half + i] = 1.0
    head = np.stack([1.0 / np.minimum(np.arange(16) + 1, 2 ** (g + 1)) for g in range(G)]).astype(np.float32)
    consts = np.concatenate([eye, rot, np.tile(head.reshape(1, -1), (P, 1))], axis=1)
    inv = (np.float32(500000.0) ** (-np.arange(0, 2 * half, 2, dtype=np.float32) / np.float32(2 * half))).astype(np.float32)
    pos = np.concatenate([np.arange(SEQ), PAST + np.arange(DEC)]).astype(np.float32)
    angle = (pos[None, :] * inv[:, None]).astype(np.float32).astype(np.float64)
    tables = np.zeros((P, 2, SEQ + DEC), np.float32)
    tables[:, 0, :] = 1.0
    for at in range(0, P, half):
        if at % HD < 2 * half:
            tables[at:at + half, 0, :] = np.cos(angle)
            tables[at:at + half, 1, :] = np.sin(angle)
    return consts, tables


def unit_layout(w_in, w_pool, w_attn_up, w_out, w_up, w_down):
    def tile(w, cols):
        rows = w.shape[0] // P
        return w[:, cols].reshape(rows, P, P).transpose(1, 0, 2).reshape(P, rows * P)

    def cols(at):
        return np.arange(at, at + P)

    q0, k0 = G * P, G * P + NJ * KV * HD
    gp0 = k0 + 2 * P
    ga0 = gp0 + D
    pooled = w_pool.transpose(1, 0, 2).reshape(P, 2 * G * P)
    up_rows = w_attn_up.reshape(KV, NJ, HD, D).transpose(1, 0, 2, 3).reshape(NJ * P, D)
    q_cols = lambda j: np.concatenate([np.arange(q0 + (g * NJ + j) * HD, q0 + (g * NJ + j + 1) * HD) for g in range(KV)])
    make = {
        "qkv": lambda m: tile(w_in, q_cols(m) if m < NJ else cols(k0 + (m - NJ) * P)),
        "xp": lambda m: tile(w_in, cols(m * P)),
        "gp": lambda m: tile(w_in, cols(gp0 + m * P)),
        "ga": lambda m: tile(w_in, cols(ga0 + m * P)),
        "ao": lambda m: tile(up_rows, cols(m * P)),
        "pool": lambda m: pooled[:, m * P:(m + 1) * P],
        "out": lambda m: tile(w_out, cols(m * P)),
    }
    units = []
    for kind, m in MIXER:
        parts = [make[kind](m)] + ([make["pool"](m)] if kind == "ao" else [])
        units.append(np.concatenate(parts + [np.zeros((P, WIDTH - sum(p.shape[1] for p in parts)), np.float32)], axis=1))
    for q in range(NQ):
        units += [tile(w_up, cols(q * D + m * P)) for m in range(KD)]
        units += [tile(w_down[q * D:(q + 1) * D], cols(m * P)) for m in range(KD)]
    return np.ascontiguousarray(np.stack(units))


def feature_major(x):
    return np.ascontiguousarray(x.T.reshape(KD, P, -1).transpose(1, 0, 2))


def token_major(y):
    return y.transpose(1, 0, 2).reshape(D, -1).T


def kernel(x_prompt, x_sample, cache_k, cache_v, state_pool, norm_mix, w_in, sinks, w_pool, pool_scale,
           w_attn_up, w_out, norm_mlp, w_up, w_down, norm_final):
    import concourse.bacc as bacc
    from concourse.bass_utils import run_bass_kernel_spmd

    f32 = lambda a: np.asarray(a)
    xp, xs = f32(x_prompt)[0], f32(x_sample)[0]
    consts, tables = constants()
    by_tile = lambda v: f32(v).reshape(KD, P).T
    s = f32(sinks)[0].reshape(KV, NJ)
    rows = np.arange(P)
    sink_cols = [s[g, 2 * pair + rows // CH] for g in range(KV) for pair in range(2)]
    sink_cols += [s[g, rows // DEC] for g in range(KV)]
    vectors = np.concatenate([by_tile(norm_mix[0]), by_tile(pool_scale[0]), by_tile(norm_mlp[0]), by_tile(norm_final),
                              np.stack(sink_cols, axis=1)], axis=1)
    ck, cv = (f32(c)[0, 0].reshape(CACHE, P) for c in (cache_k, cache_v))
    hist = f32(state_pool)[0, 0].T.reshape(G, P, PBUF).transpose(1, 0, 2)
    arrays = {
        "x0": feature_major(np.concatenate([xp[:TB], xs])),
        "x123": np.stack([feature_major(xp[b * TB:(b + 1) * TB]) for b in range(1, NB)]),
        "weights": unit_layout(*(f32(w)[0] for w in (w_in, w_pool, w_attn_up, w_out, w_up, w_down))),
        "consts": consts, "vectors": vectors, "tables": tables,
        "state_s": np.concatenate([np.zeros((P, G, 1), np.float32), hist], axis=2),
        "kcache_t": ck[CACHE - CH:].T, "vcache": cv[CACHE - CH:],
        "kold": ck[DEC:], "vold": cv[DEC:],
    }
    arrays = {n: np.ascontiguousarray(a) for n, a in arrays.items()}
    outs = {"y0": (P, KD, CMAX), "y123": (NB - 1, P, KD, TB), "k_new": (P, P), "v_new": (P, P), "p_new": (P, G, 16),
            "k_old_out": (CACHE - DEC, P), "v_old_out": (CACHE - DEC, P), "ks_new": (P, DEC), "vs_new": (DEC, P),
            "ps_new": (P, G, 16)}
    nc = bacc.Bacc("TRN2", target_bir_lowering=False, num_devices=1)
    args = [nc.dram_tensor(n, a.shape, F32, kind="ExternalInput").ap() for n, a in arrays.items()]
    args += [nc.dram_tensor(n, shape, F32, kind="ExternalOutput").ap() for n, shape in outs.items()]
    build(nc, *args)
    got = run_bass_kernel_spmd(nc, [arrays], core_ids=[0]).results[0]

    first = token_major(got["y0"])
    rest = [token_major(got["y123"][b]) for b in range(NB - 1)]
    heads = lambda a: np.ascontiguousarray(a).reshape(1, 1, CACHE, KV, HD)
    tail = lambda a: np.ascontiguousarray(a[:, :, 1:].transpose(2, 1, 0)).reshape(1, 1, PBUF, G * P)
    return (np.concatenate([first[:TB], *rest])[None], first[TB:][None],
            heads(got["k_new"].T), heads(got["v_new"]), tail(got["p_new"]),
            heads(np.concatenate([got["k_old_out"], got["ks_new"].T])),
            heads(np.concatenate([got["v_old_out"], got["vs_new"]])),
            tail(got["ps_new"]))
```

```python
from contextlib import ExitStack

import numpy as np
import concourse.bass as bass
from concourse import mybir

F32 = mybir.dt.float32
F32R = mybir.dt.float32r
ALU = mybir.AluOpType
ACT = mybir.ActivationFunctionType
AX = mybir.AxisListType.X

P = 128
D = 1024
KD = D // P
SEQ, DEC = 2048, 32
TB = 512
NB = SEQ // TB
CH = 64
NC = TB // CH
NT = TB // P
HD = 64
NJ = 4
KV = 2
G = 4
PBUF = 15
PAST = 2048
CACHE = 128
DFF = 4096
NQ = DFF // D
WIDTH = P * KD
CMAX = TB + DEC
XW = 16 + TB
XWMAX = XW + 16 + DEC
KEYS_S = DEC + CH
EPS = 1e-6
SCALE = HD ** -0.5
MASKED = -1e30



def mixer_plan():
    plan = [("qkv", m) for m in range(6)] + [("xp", m) for m in range(G)] + [("gp", m) for m in range(KD)]
    for m in range(KD):
        plan += [("ga", m), ("ao", m)]
    return plan + [("out", m) for m in range(KD)]


MIXER = mixer_plan()
M_MLP = len(MIXER)
UNITS = M_MLP + 2 * KD * NQ
AO_WIDTH = (NJ + 1) * P
RAW, SPLIT = 4, 2
assert UNITS % 2 == 0 and M_MLP % 2 == 0 and 2 * KD % RAW == 0
ROPE_LOAD = 16
K_HALF = TB // 2 + CH
ROT = HD // 4
PARTNERS = [(p + ROT // 2) % ROT if p < ROT else p for p in range(32)]
Y_STORES = (2, 3, 4, 5)
POOL_STEPS = (8, 10, 12, 15)
STATE_STEP = 20
POOLED = KD - G
ATT0 = 7


def build(nc, x0, x123, weights, consts, vectors, tables, state_s, kcache_t, vcache, kold, vold,
          y0, y123, k_new, v_new, p_new, k_old_out, v_old_out, ks_new, vs_new, ps_new):
    with ExitStack() as ctx:
        def sb(name, shape, dt=F32):
            return ctx.enter_context(nc.sbuf_tensor(name, shape, dt))

        def sem(name):
            return ctx.enter_context(nc.semaphore(name))

        class Signal:

            def __init__(self, name, items):
                self.sem = sem(name)
                self.count = {item: n + 1 for n, item in enumerate(items)}

        def cols(b):
            return CMAX if b == 0 else TB

        def nchunks(b):
            return NC + 1 if b == 0 else NC

        xT = sb("xT", [P, KD, CMAX])
        hT = sb("hT", [P, KD, CMAX])
        nH, nL = sb("nH", [P, KD, CMAX], F32R), sb("nL", [P, KD, CMAX], F32R)
        midH, midL = sb("midH", [P, KD, CMAX], F32R), sb("midL", [P, KD, CMAX], F32R)
        attH, attL = sb("attH", [P, NJ, CMAX], F32R), sb("attL", [P, NJ, CMAX], F32R)
        qbuf = sb("qbuf", [P, NJ * CMAX])
        qC = qbuf[:, 0:NJ * TB].rearrange("p (c j n) -> p c j n", c=NC, j=NJ)
        qS = qbuf[:, NJ * TB:].rearrange("p (j n) -> p j n", j=NJ)
        kT = sb("kT", [P, 2 * K_HALF + DEC])
        k_before = kT[:, TB // 2:K_HALF]
        k_halves = kT[:, 0:2 * K_HALF].rearrange("p (s n) -> p s n", s=2)
        k_chunks = k_halves[:, :, 0:TB // 2].rearrange("p s (t n) -> p t s n", n=CH)
        vA = sb("vA", [P, NT, P])
        vB = sb("vB", [P, NT + 1, P])
        vS = sb("vS", [KEYS_S, P])
        kcT = sb("kcT", [P, CH])
        raw = sb("raw", [P, RAW, WIDTH])
        wH, wL = sb("wH", [P, SPLIT, WIDTH], F32R), sb("wL", [P, SPLIT, WIDTH], F32R)
        work = sb("work", [P, 3, CMAX])
        sq = sb("sq", [P, 2, XWMAX])
        acc = sb("acc", [P, CMAX])
        diff = sb("diff", [P, XWMAX])
        xb = sb("xb", [P, 3, XWMAX])
        carry = sb("carry", [P, G, 16])
        carry_s = sb("carry_s", [P, G, 16])
        state = sb("state", [P, G, 16])
        pr = sb("pr", [P, 2, 4 * P])
        prT = sb("prT", [P, 2, 4 * P])
        rope = sb("rope", [P, 2, CMAX])
        rms = sb("rms", [P, CMAX])
        cst = sb("cst", [P, P + G * 16])
        ident = cst[:, 0:P]
        head_scale = cst[:, P:].rearrange("p (g c) -> p g c", g=G)
        ones = sb("ones", [P, P])
        vec = sb("vec", [P, 4 * KD + 6])
        g_mix, p_scale, g_mlp, g_fin = (vec[:, i * KD:(i + 1) * KD] for i in range(4))
        nsink = sb("nsink", [P, 6])
        eps_tile = sb("eps", [P, 1])
        eps = eps_tile[:, :]
        columns = sb("columns", [P, 7, 4])
        smax, negm, sinkd, esink, rsum, den, rden = (columns[:, i, :] for i in range(7))

        prod = [ctx.enter_context(nc.psum_tensor(f"prod{i}", [P, 2, 512], F32)) for i in range(2)]
        auxA = ctx.enter_context(nc.psum_tensor("auxA", [P, 2, 512], F32))
        auxB = ctx.enter_context(nc.psum_tensor("auxB", [P, 2, 512], F32))

        def pview(t, b):
            return t[:, 0:2, 0:CMAX // 2] if b == 0 else t[:, 0:1, 0:TB]

        def sview(ap, b):
            return ap[:, 0:cols(b)].rearrange("p (s n) -> p s n", s=2 if b == 0 else 1)

        def f(ap):
            return ap.bitcast(F32)

        raw_in = [sem(f"raw_in{i}") for i in range(RAW)]
        vec_in, const_in, x_in = sem("vec_in"), sem("const_in"), sem("x_in")
        rope_in, sample_in = sem("rope_in"), sem("sample_in")
        x_first = [sem(f"x_first{i}") for i in range(KD)]
        y_out = [sem(f"y_out{i}") for i in range(KD // 2)]
        kv_out, pool_out, copy_out = sem("kv_out"), sem("pool_out"), sem("copy_out")
        start = sem("start")
        w_high, w_low = sem("w_high"), sem("w_low")
        prod_done = sem("prod_done")
        relu_done, hid_sq = sem("relu_done"), sem("hid_sq")
        hid_high, hid_low = sem("hid_high"), sem("hid_low")
        down_added = sem("down_added")
        vec_chain, pool_chain = sem("vec_chain"), sem("pool_chain")

        norms = [("x", 0)]
        for b in range(NB):
            norms += [("h", b)] + ([("x", b + 1)] if b + 1 < NB else []) + [("f", b)]
        inner = [n for n in norms if n[0] != "f"]
        blocks = range(NB)
        s_sq = Signal("squared", [(*n, k) for n in norms for k in range(KD)])
        s_acc = Signal("squares_added", [(*n, k) for n in norms for k in range(1, KD)])
        s_sum = Signal("squares_summed", norms)
        s_root = Signal("root_taken", norms)
        s_r = Signal("root_inverted", norms)
        s_nH = Signal("gained_high", [(*n, k) for n in inner for k in range(KD)])
        s_nL = Signal("gained_low", [(*n, k) for n in inner for k in range(KD)])
        s_tab = Signal("angles_scaled", [(b,) for b in blocks])
        s_fg = Signal("final_gained", [(b, k) for b in blocks[:-1] for k in range(KD)])
        s_y = Signal("y_normed", [(b, k) for b in blocks for k in range(KD)])
        s_tmp = Signal("qk_copied", [(b, i) for b in blocks for i in range(NJ + 1)])
        s_vn = Signal("v_normed", [(b,) for b in blocks])
        s_q = Signal("rotated", [(b, i) for b in blocks for i in range(5)])
        s_vt = Signal("v_transposed", [(b,) for b in blocks])
        s_vA = Signal("vA_copied", [(b,) for b in blocks])
        s_vB = Signal("vB_copied", [(b,) for b in blocks])
        groups = [(b, g) for b in blocks for g in range(G)]
        s_xb = Signal("pool_in_copied", groups)
        s_carry = Signal("pool_carried", groups)
        s_p = Signal("pooled", groups)
        s_pH = Signal("pooled_high", groups)
        s_pL = Signal("pooled_low", groups)
        chunks = [(b, c) for b in blocks for c in range(nchunks(b))]
        s_sc = Signal("scores", chunks)
        s_negm = Signal("max_negated", chunks)
        s_exp = Signal("exps", chunks)
        s_prn = Signal("probs_normed", chunks)
        s_pt = Signal("probs_transposed", chunks)
        s_ptS = Signal("probs_copied", chunks)
        s_pv = Signal("values_mixed", chunks)
        s_aH = Signal("attn_high", chunks)
        s_aL = Signal("attn_low", chunks)
        tiles = [(b, m) for b in blocks for m in range(KD)]
        s_gz = Signal("gate_scaled", [(b, kind, m) for b in blocks for kind in ("gp", "ga") for m in range(KD)])
        s_gp = Signal("pool_gate", tiles)
        s_pp = Signal("pool_up", tiles)
        s_pool = Signal("pool_gated", tiles)
        s_ga = Signal("attn_gate", tiles)
        s_gat = Signal("attn_gated", tiles)
        s_mrg = Signal("merged", tiles)
        s_mH = Signal("merged_high", tiles)
        s_mL = Signal("merged_low", tiles)
        s_h = Signal("h_added", tiles)

        def wait(eng, signal, *item):
            eng.wait_ge(signal.sem, signal.count[item])

        def unit_width(u):
            return AO_WIDTH if u < M_MLP and MIXER[u][0] == "ao" else WIDTH

        def wait_product(eng, b, i):
            eng.wait_ge(prod_done, b * UNITS + i + 1)

        def wait_mlp(eng, b, q, i):
            eng.wait_ge(prod_done, 16 * q + (b * UNITS + M_MLP + i + 1))

        def hid(b, q, m):
            return 8 * q + (b * KD * NQ + m + 1)

        def quarters(eng, b, up, down, last):
            up(b, 0)
            with eng.Fori(0, NQ - 1) as q:
                down(b, q)
                up(b, q + 1)
            last(b)

        def inverse(kind):
            return acc if kind == "f" else rms

        def squares(kind, b, k):
            return hT[:, k, :] if (kind, b) == ("x", 0) else sq[:, k % 2, :]

        block = ctx.enter_context(nc.Block())

        @block.sync
        def _(sp):
            def load_mixer_unit(b, u):
                n = b * UNITS + u
                if n >= RAW:
                    sp.wait_ge(w_low, n - RAW + 1)
                w = unit_width(u)
                sp.dma_start(raw[:, n % RAW, 0:w], weights[u, :, 0:w]).then_inc(raw_in[n % RAW], 16)

            def load_mlp_unit(b, q, i):
                sp.wait_ge(w_low, 16 * q + (b * UNITS + M_MLP + i - RAW + 1))
                slot = (b * UNITS + M_MLP + i) % RAW
                sp.dma_start(raw[:, slot, :], weights[16 * q + (M_MLP + i), :, :]).then_inc(raw_in[slot], 16)

            def load_rope(b):
                if b > 0:
                    wait(sp, s_q, b - 1, NJ)
                sp.dma_start(rope[:, :, 0:TB], tables[:, :, b * TB:(b + 1) * TB]).then_inc(rope_in, 16)
                if b == 0:
                    sp.dma_start(rope[:, :, TB:CMAX], tables[:, :, SEQ:SEQ + DEC]).then_inc(rope_in, 16)

            sp.dma_start(vec[:, :], vectors).then_inc(vec_in, 16)
            load_mixer_unit(0, 0)
            for k in range(KD):
                sp.dma_start(xT[:, k, :], x0[:, k, :]).then_inc(x_first[k], 16)
            load_mixer_unit(0, 1)
            sp.dma_start(cst[:, :], consts).then_inc(const_in, 16)
            load_mixer_unit(0, 2)
            load_rope(0)
            load_mixer_unit(0, 3)
            sp.dma_start(kcT[:, :], kcache_t).then_inc(sample_in, 16)
            sp.dma_start(vS[DEC:KEYS_S, :], vcache).then_inc(sample_in, 16)
            sp.dma_start(state[:, :, :], state_s).then_inc(sample_in, 16)
            sp.dma_start(k_old_out, kold).then_inc(copy_out, 16)
            sp.dma_start(v_old_out, vold).then_inc(copy_out, 16)

            def up(b, q):
                for m in range(KD):
                    load_mlp_unit(b, q, m)
                    if isinstance(q, int) and m == 3 and b + 1 < NB:
                        wait(sp, s_h, b, KD - 1)
                        sp.dma_start(xT[:, :, 0:TB], x123[b, :, :, :]).then_inc(x_in, 16)

            def down(b, q):
                for m in range(KD):
                    load_mlp_unit(b, q, KD + m)

            for b in blocks:
                for u in range(RAW if b == 0 else 0, M_MLP):
                    load_mixer_unit(b, u)
                    if u == ROPE_LOAD and b + 1 < NB:
                        load_rope(b + 1)
                quarters(sp, b, up, down, lambda b: down(b, NQ - 1))
            sp.wait_ge(copy_out, 32)

        @block.tensor
        def _(pe):
            def stream(out, b, lhs, rhs, first, last):
                for s, lo, hi in ((0, 0, 272), (1, 272, CMAX)) if b == 0 else ((0, 0, TB),):
                    ins = nc.tensor.matmul(out[:, s, 0:hi - lo], lhs, rhs[:, lo:hi], start=first, stop=last)
                return ins

            def three(out, b, uslot, off, high, low, k, first, last):
                wh, wl = wH[:, uslot, off:off + P], wL[:, uslot, off:off + P]
                stream(out, b, wh, high[:, k, :], first, False)
                stream(out, b, wh, low[:, k, :], False, False)
                return stream(out, b, wl, high[:, k, :], False, last)

            def product(b, slot, high, low, nk, before_k=None):
                for k in range(nk):
                    if before_k:
                        before_k(k)
                    ins = three(prod[slot], b, slot, k * P, high, low, k, k == 0, k == nk - 1)
                ins.then_inc(prod_done, 1)

            def wait_read(b, i):
                if i < 2:
                    if b > 0:
                        pe.wait_ge(down_added, hid(b - 1, NQ - 1, KD - 2 + i))
                    return
                kind, m = MIXER[i - 2]
                signal = {"qkv": s_tmp, "xp": s_xb, "gp": s_gz, "ga": s_gz, "ao": s_gat, "out": s_h}[kind]
                if (kind, m) == ("qkv", NJ + 1):
                    wait(pe, s_vn, b)
                else:
                    wait(pe, signal, b, *((kind, m) if signal is s_gz else (m,)))

            def mixer_product(b, i):
                kind, m = MIXER[i]
                pe.wait_ge(w_low, b * UNITS + i + 1)
                high, low, nk = {"ao": (attH, attL, NJ), "out": (midH, midL, KD)}.get(kind, (nH, nL, KD))
                if kind == "ao":
                    if m == 0:
                        wait(pe, s_aL, b, nchunks(b) - 1)
                    else:
                        wait(pe, s_pool, b, m - 1)
                    g = m // 2
                    wait(pe, s_pL, b, g)
                    three(auxB, b, i % 2, NJ * P, midH, midL, POOLED + g, True, True).then_inc(s_pp.sem, 1)
                wait_read(b, i)

                def before(k):
                    if i == 0:
                        wait(pe, s_nL, "x", b, k)
                    if kind == "out" and m == 0:
                        wait(pe, s_mL, b, k)
                    if (b, i, k) == (0, 1, 6):
                        sum_squares("x", 0)
                    if b > 0 and (i, k) == (1, 0):
                        sum_squares("f", b - 1)
                product(b, i % 2, high, low, nk, before)

            def sum_squares(kind, b):
                wait(pe, s_acc, kind, b, KD - 1)
                if (kind, b) == ("x", 0):
                    pe.wait_ge(start, 1)
                if kind == "f" and b + 1 < NB:
                    wait(pe, s_root, "x", b + 1)
                stream(auxA, b, ones[:, :], acc, True, True).then_inc(s_sum.sem, 1)

            def transpose_v(b):
                wait(pe, s_vn, b)
                if b > 0:
                    wait(pe, s_root, "f", b - 1)
                else:
                    wait(pe, s_root, "x", b)
                    pe.wait_ge(const_in, 16)
                for t in range(NT):
                    ins = nc.tensor.transpose(auxA[:, 1, t * P:(t + 1) * P], work[:, 1, t * P:(t + 1) * P], ident)
                if b == 0:
                    ins = nc.tensor.transpose(auxA[0:DEC, 0, 0:P], work[:, 1, TB:CMAX], ident)
                ins.then_inc(s_vt.sem, 1)

            def scores(b, c):
                if c >= 1:
                    wait(pe, s_exp, b, c - 1)
                else:
                    wait(pe, s_q, b, 4)
                    wait(pe, s_vA, b)
                if c == NC:
                    pe.wait_ge(sample_in, 48)
                for g in range(KV):
                    rows, bank = slice(g * HD, (g + 1) * HD), auxA[:, g, :]
                    if c == NC:
                        q = qbuf[rows, NJ * TB:]
                        nc.tensor.matmul(bank[:, 0:DEC], q, kT[rows, 2 * K_HALF:],
                                         start=True, stop=True)
                        ins = nc.tensor.matmul(bank[:, DEC:KEYS_S], q, kcT[rows, :],
                                               start=True, stop=True)
                        continue
                    for pair in range(2):
                        at = pair * P
                        q = qbuf[rows, (4 * c + 2 * pair) * CH:(4 * c + 2 * pair + 2) * CH]
                        step, t = (K_HALF, c // 2) if c % 2 else (TB // 2, c // 2)
                        keys = kT[rows, 0:2 * step].rearrange("p (s n) -> p s n", s=2)
                        ins = nc.tensor.matmul(bank[:, at:at + P], q, keys[:, :, t * CH:(t + 1) * CH],
                                               start=True, stop=True)
                ins.then_inc(s_sc.sem, 1)

            def transpose_probs(b, c):
                wait(pe, s_prn, b, c)
                if c >= 1:
                    wait(pe, s_ptS, b, c - 1)
                if c == NC:
                    for g in range(KV):
                        ins = nc.tensor.transpose(auxB[0:KEYS_S, 1, g * P:(g + 1) * P],
                                                  pr[:, 0, g * KEYS_S:(g + 1) * KEYS_S], ident)
                else:
                    for i in range(4):
                        ins = nc.tensor.transpose(auxB[:, 1, i * P:(i + 1) * P], pr[:, c % 2, i * P:(i + 1) * P], ident)
                ins.then_inc(s_pt.sem, 1)

            def mix_values(b, c):
                wait(pe, s_ptS, b, c)
                if c >= 1:
                    wait(pe, s_aL, b, c - 1)
                else:
                    wait(pe, s_vB, b)
                for g in range(KV):
                    feats = slice(g * HD, (g + 1) * HD)
                    if c == NC:
                        ins = nc.tensor.matmul(auxB[feats, 0, 0:P], vS[:, feats], prT[0:KEYS_S, 0, g * P:(g + 1) * P],
                                               start=True, stop=True)
                    else:
                        v = vA if c % 2 else vB
                        ins = nc.tensor.matmul(auxB[feats, 0, 0:2 * P], v[:, c // 2, feats],
                                               prT[:, c % 2, 2 * g * P:2 * (g + 1) * P], start=True, stop=True)
                ins.then_inc(s_pv.sem, 1)

            def between(b, i):
                if i == 6:
                    transpose_v(b)
                if 0 <= i - ATT0 - 2 < nchunks(b):
                    mix_values(b, i - ATT0 - 2)
                if 0 <= i - ATT0 - 1 < nchunks(b):
                    transpose_probs(b, i - ATT0 - 1)
                if 0 <= i - ATT0 < nchunks(b):
                    scores(b, i - ATT0)

            def up(b, q):
                for m in range(KD):
                    first = isinstance(q, int) and q == 0
                    if m >= 2:
                        pe.wait_ge(relu_done, hid(b, q, m - 2))
                    elif first:
                        wait(pe, s_h, b, KD - 2 + m)
                    else:
                        pe.wait_ge(down_added, hid(b, q - 1, KD - 2 + m))
                    pe.wait_ge(w_low, 16 * q + (b * UNITS + M_MLP + m + 1))

                    def before(k):
                        if first and m == 0:
                            wait(pe, s_nL, "h", b, k)
                        if first and (m, k) == (0, 6):
                            sum_squares("h", b)
                    product(b, m % 2, nH, nL, KD, before)

            def down(b, q):
                for m in range(KD):
                    if m >= 2:
                        pe.wait_ge(down_added, hid(b, q, m - 2))
                    else:
                        pe.wait_ge(relu_done, hid(b, q, KD - 2 + m))
                    pe.wait_ge(w_low, 16 * q + (b * UNITS + M_MLP + KD + m + 1))
                    before = (lambda k: pe.wait_ge(hid_low, hid(b, q, k))) if m == 0 else None
                    product(b, m % 2, midH, midL, KD, before)
                    if isinstance(q, int) and q == NQ - 1 and b + 1 < NB:
                        if m == 0:
                            sum_squares("x", b + 1)

            for b in blocks:
                for i in range(M_MLP):
                    mixer_product(b, i)
                    between(b, i)
                quarters(pe, b, up, down, lambda b: down(b, NQ - 1))
            sum_squares("f", NB - 1)

        @block.scalar
        def _(act):
            def copy(out, in_, scale=1.0):
                return nc.scalar.activation(out, in_, ACT.Copy, scale=scale)

            def split_high(b, u):
                n = b * UNITS + u
                if n >= NB * UNITS:
                    return
                w = unit_width(u % UNITS)
                act.wait_ge(raw_in[n % RAW], 16 * (n // RAW + 1))
                copy(wH[:, n % 2, 0:w], raw[:, n % RAW, 0:w]).then_inc(w_high, 1)

            def split_high_mlp(b, q, i):
                n = b * UNITS + M_MLP + i
                act.wait_ge(raw_in[n % RAW], 64 * q + 16 * (n // RAW + 1))
                copy(wH[:, n % 2, :], raw[:, n % RAW, :]).then_inc(w_high, 1)

            def square(kind, b, k, src):
                at = norms.index((kind, b))
                if at and k >= 2:
                    wait(act, s_acc, kind, b, max(1, k - 2))
                elif at:
                    wait(act, s_acc, *norms[at - 1], KD - 1)
                nc.scalar.activation(sview(squares(kind, b, k), b), sview(src[:, k, :], b), ACT.Square).then_inc(s_sq.sem, 1)

            def root(kind, b):
                wait(act, s_sum, kind, b)
                nc.scalar.activation(sview(inverse(kind), b), pview(auxA, b), ACT.Sqrt, bias=eps,
                                     scale=1.0 / D).then_inc(s_root.sem, 1)

            def gained_high(kind, b, k):
                src, gain = (xT, g_mix) if kind == "x" else (hT, g_mlp)
                copy(nH[:, k, 0:cols(b)], src[:, k, 0:cols(b)], gain[:, k:k + 1]).then_inc(s_nH.sem, 1)

            def exps(b, c):
                wait(act, s_negm, b, c)
                n, w = (KV, KEYS_S) if c == NC else (4, P)
                for i in range(n):
                    at = i % (n // KV) * w
                    nc.scalar.activation(pr[:, c % 2, i * w:(i + 1) * w], auxA[:, i * KV // n, at:at + w], ACT.Exp,
                                         bias=negm[:, i:i + 1], scale=SCALE, accum_out=rsum[:, i:i + 1])
                nc.scalar.activation(esink[:, 0:n], sinkd[:, 0:n], ACT.Exp).then_inc(s_exp.sem, 1)

            def copy_probs(b, c):
                wait(act, s_pt, b, c)
                if c == NC:
                    copy(prT[0:KEYS_S, 0, 0:2 * P], auxB[0:KEYS_S, 1, 0:2 * P]).then_inc(s_ptS.sem, 1)
                else:
                    copy(prT[:, c % 2, :], auxB[:, 1, :]).then_inc(s_ptS.sem, 1)

            def attn_high(b, c):
                wait(act, s_pv, b, c)
                w = DEC if c == NC else CH
                copy(attH[:, :, c * CH:c * CH + w],
                     auxB[:, 0, 0:NJ * w].rearrange("p (j n) -> p j n", j=NJ)).then_inc(s_aH.sem, 1)

            def merged_high(b, m):
                wait(act, s_mrg, b, m)
                copy(midH[:, m, 0:cols(b)], hT[:, m, 0:cols(b)], 0.5).then_inc(s_mH.sem, 1)

            def pooled_high(b, g):
                wait(act, s_p, b, g)
                ins = copy(midH[:, POOLED + g, 0:TB], diff[:, 16:XW])
                if b == 0:
                    ins = copy(midH[:, POOLED + g, TB:CMAX], diff[:, XWMAX - DEC:XWMAX])
                ins.then_inc(s_pH.sem, 1)

            def store_y(b, part):
                wait(act, s_y, b, 2 * part + 1)
                ks = slice(2 * part, 2 * part + 2)
                dst = y0[:, ks, :] if b == 0 else y123[b - 1, :, ks, :]
                act.dma_start(dst, hT[:, ks, 0:cols(b)]).then_inc(y_out[part], 16)

            def step(b, i):
                kind, m = MIXER[i]
                if (b, i) == (0, 1):
                    root("x", 0)
                wait_product(act, b, i)
                split_high(b, i + 2)
                if kind == "qkv" and m <= NJ:
                    if m >= 2:
                        wait(act, s_q, b, m - 2)
                    copy(sview(work[:, m % 2, :], b), pview(prod[i % 2], b)).then_inc(s_tmp.sem, 1)
                if kind == "gp":
                    wait(act, s_gz, b, "gp", m)
                    gate = hT[:, m, 0:cols(b)]
                    nc.scalar.activation(gate, gate, ACT.Tanh, scale=0.5).then_inc(s_gp.sem, 1)
                if kind == "ga":
                    wait(act, s_gz, b, "ga", m)
                    gate = work[:, m % 2, 0:cols(b)]
                    nc.scalar.activation(gate, gate, ACT.Tanh, scale=0.5).then_inc(s_ga.sem, 1)
                if kind == "ao":
                    merged_high(b, m)
                if kind == "out":
                    wait(act, s_h, b, m)
                    gained_high("h", b, m)
                    square("h", b, m, hT)
                if b > 0 and i == 0:
                    root("f", b - 1)
                if b > 0 and i in Y_STORES:
                    store_y(b - 1, Y_STORES.index(i))
                if i == 6:
                    wait(act, s_vt, b)
                    if b == 0:
                        copy(vS[0:DEC, :], auxA[0:DEC, 0, 0:P])
                    copy(vA[:, :, :], auxA[:, 1, :].rearrange("p (t f) -> p t f", t=NT)).then_inc(s_vA.sem, 1)
                    if b in (0, NB - 1):
                        wait(act, s_q, b, NJ)
                        wait(act, s_vA, b)
                    if b == 0:
                        act.dma_start(ks_new, kT[:, 2 * K_HALF:]).then_inc(kv_out, 16)
                        act.dma_start(vs_new, vS[0:DEC, :]).then_inc(kv_out, 16)
                    if b == NB - 1:
                        act.dma_start(k_new, k_halves[:, :, TB // 2 - CH:TB // 2]).then_inc(kv_out, 16)
                        act.dma_start(v_new, vA[:, NT - 1, :]).then_inc(kv_out, 16)
                if 0 <= i - ATT0 - 2 < nchunks(b):
                    attn_high(b, i - ATT0 - 2)
                if 0 <= i - ATT0 - 1 < nchunks(b):
                    copy_probs(b, i - ATT0 - 1)
                if 0 <= i - ATT0 < nchunks(b):
                    exps(b, i - ATT0)
                if i in POOL_STEPS:
                    pooled_high(b, POOL_STEPS.index(i))
                if i == STATE_STEP and b in (0, NB - 1):
                    wait(act, s_carry, b, G - 1)
                    if b == 0:
                        act.dma_start(ps_new, carry_s[:, :, :]).then_inc(pool_out, 16)
                    else:
                        act.dma_start(p_new, carry[:, :, :]).then_inc(pool_out, 16)

            def up(b, q):
                first = isinstance(q, int) and q == 0
                for m in range(KD):
                    wait_mlp(act, b, q, m)
                    split_high_mlp(b, q, m + 2)
                    act.wait_ge(relu_done, hid(b, q, m))
                    nc.scalar.activation(midH[:, m, 0:cols(b)], work[:, m % 2, 0:cols(b)], ACT.Square).then_inc(hid_high, 1)
                    if first and b + 1 < NB and m >= 4:
                        if m == 4:
                            act.wait_ge(x_in, 16 * (b + 1))
                        square("x", b + 1, 2 * m - 8, xT)
                        square("x", b + 1, 2 * m - 7, xT)

            def down(b, q):
                for m in range(KD):
                    wait_mlp(act, b, q, KD + m)
                    split_high_mlp(b, q, KD + m + 2)

            def last_down(b):
                for m in range(KD):
                    wait_mlp(act, b, NQ - 1, KD + m)
                    split_high(b, UNITS - KD + m + 2)
                    if b + 1 < NB:
                        gained_high("x", b + 1, m)
                        if m == 0:
                            root("x", b + 1)
                    act.wait_ge(down_added, hid(b, NQ - 1, m))
                    square("f", b, m, hT)
                    if b + 1 < NB:
                        wait(act, s_sq, "f", b, m)
                        copy(hT[:, m, 0:cols(b)], hT[:, m, 0:cols(b)], g_fin[:, m:m + 1]).then_inc(s_fg.sem, 1)

            split_high(0, 0)
            act.wait_ge(vec_in, 16)
            for k in range(KD):
                act.wait_ge(x_first[k], 16)
                gained_high("x", 0, k)
            split_high(0, 1)
            for k in range(KD):
                square("x", 0, k, xT)
            act.wait_ge(start, 1)
            for b in blocks:
                for i in range(M_MLP):
                    step(b, i)
                root("h", b)
                quarters(act, b, up, down, last_down)
            root("f", NB - 1)
            for part in range(KD // 2):
                store_y(NB - 1, part)
            for part in range(KD // 2):
                act.wait_ge(y_out[part], 16 * NB)
            act.wait_ge(kv_out, 64)
            act.wait_ge(pool_out, 32)

        @block.vector
        def _(dve):
            tt, stt = nc.vector.tensor_tensor, nc.vector.scalar_tensor_tensor
            chain = [0]

            def link(ins):
                chain[0] += 1
                ins.then_inc(vec_chain, 1)
                dve.wait_ge(vec_chain, chain[0])

            def low(out, x, high):
                return tt(out, x, f(high), ALU.subtract)

            def split_low(b, u):
                n = b * UNITS + u
                if n >= NB * UNITS:
                    return
                w = unit_width(u % UNITS)
                dve.wait_ge(w_high, n + 1)
                low(wL[:, n % 2, 0:w], raw[:, n % RAW, 0:w], wH[:, n % 2, 0:w]).then_inc(w_low, 1)

            def split_low_mlp(b, q, i):
                n = b * UNITS + M_MLP + i
                dve.wait_ge(w_high, 16 * q + (n + 1))
                low(wL[:, n % 2, :], raw[:, n % RAW, :], wH[:, n % 2, :]).then_inc(w_low, 1)

            def add_square(kind, b, k):
                wait(dve, s_sq, kind, b, k)
                n = cols(b)
                if k == 1:
                    tt(acc[:, 0:n], squares(kind, b, 0)[:, 0:n], squares(kind, b, 1)[:, 0:n], ALU.add).then_inc(s_acc.sem, 1)
                elif k > 1:
                    wait(dve, s_acc, kind, b, k - 1)
                    tt(acc[:, 0:n], acc[:, 0:n], squares(kind, b, k)[:, 0:n], ALU.add).then_inc(s_acc.sem, 1)

            def invert(kind, b):
                r = inverse(kind)[:, 0:cols(b)]
                wait(dve, s_root, kind, b)
                nc.vector.reciprocal(r, r).then_inc(s_r.sem, 1)

            def gained_low(kind, b, k):
                src, gain = (xT, g_mix) if kind == "x" else (hT, g_mlp)
                wait(dve, s_nH, kind, b, k)
                n = cols(b)
                stt(out=nL[:, k, 0:n], in0=src[:, k, 0:n], scalar=gain[:, k:k + 1], in1=f(nH[:, k, 0:n]),
                    op0=ALU.mult, op1=ALU.subtract).then_inc(s_nL.sem, 1)

            def scale_angles(b):
                dve.wait_ge(rope_in, 16 * (b + 2))
                wait(dve, s_r, "x", b)
                table = rope[:, :, 0:cols(b)]
                tt(table, table, rms[:, 0:cols(b)].unsqueeze(1).to_broadcast([P, 2, cols(b)]),
                   ALU.mult).then_inc(s_tab.sem, 1)

            def final(b, k):
                stt(out=hT[:, k, 0:cols(b)], in0=hT[:, k, 0:cols(b)], scalar=g_fin[:, k:k + 1],
                    in1=acc[:, 0:cols(b)], op0=ALU.mult, op1=ALU.mult).then_inc(s_y.sem, 1)

            def rotate(b, i):
                n = cols(b)
                q, partner = work[:, i % 2, :], work[:, 2, :]
                if i == 0:
                    wait(dve, s_tab, b)
                wait(dve, s_tmp, b, i)
                link(nc.vector.stream_shuffle(partner[:, 0:n], q[:, 0:n], PARTNERS))
                tt(partner[:, 0:n], partner[:, 0:n], rope[:, 1, 0:n], ALU.mult)
                link(tt(q[:, 0:n], q[:, 0:n], rope[:, 0, 0:n], ALU.mult))
                if i == NJ:
                    by_chunk = lambda ap: ap[:, 0:TB].rearrange("p (t s n) -> p t s n", s=2, n=CH)
                    ins = tt(k_chunks, by_chunk(q), by_chunk(partner), ALU.add)
                    if b == 0:
                        ins = tt(kT[:, 2 * K_HALF:], q[:, TB:CMAX], partner[:, TB:CMAX], ALU.add)
                else:
                    by_chunk = lambda ap: ap[:, 0:TB].rearrange("p (c n) -> p c n", c=NC)
                    ins = tt(qC[:, :, i, :], by_chunk(q), by_chunk(partner), ALU.add)
                    if b == 0:
                        ins = tt(qS[:, i, :], q[:, TB:CMAX], partner[:, TB:CMAX], ALU.add)
                ins.then_inc(s_q.sem, 1)
                wait(dve, s_q, b, i)

            def row_max(b, c):
                wait(dve, s_sc, b, c)
                n, w = (KV, KEYS_S) if c == NC else (4, P)
                sc = auxA[:, :, 0:n // KV * w].rearrange("p g (i k) -> p g i k", k=w)
                sink = nsink[:, 4:6] if c == NC else nsink[:, 0:4]
                if b == 0 and c == 0:
                    link(nc.vector.tensor_scalar(sc[:, :, :, CH:P], sc[:, :, :, CH:P], MASKED, None, ALU.add))
                link(nc.vector.tensor_reduce(smax[:, 0:n].rearrange("p (g i) -> p g i", g=KV), sc, AX, ALU.max))
                link(stt(out=negm[:, 0:n], in0=smax[:, 0:n], scalar=-SCALE, in1=sink, op0=ALU.mult, op1=ALU.min))
                tt(sinkd[:, 0:n], negm[:, 0:n], sink, ALU.subtract).then_inc(s_negm.sem, 1)

            def norm_probs(b, c):
                wait(dve, s_exp, b, c)
                n, w = (KV, KEYS_S) if c == NC else (4, P)
                link(tt(den[:, 0:n], rsum[:, 0:n], esink[:, 0:n], ALU.add))
                link(nc.vector.reciprocal(rden[:, 0:n], den[:, 0:n]))
                p = pr[:, c % 2, 0:n * w].rearrange("p (i k) -> p i k", i=n)
                tt(p, p, rden[:, 0:n].unsqueeze(2).to_broadcast([P, n, w]), ALU.mult).then_inc(s_prn.sem, 1)

            def attn_low(b, c):
                wait(dve, s_aH, b, c)
                w = DEC if c == NC else CH
                at = slice(c * CH, c * CH + w)
                low(attL[:, :, at], auxB[:, 0, 0:NJ * w].rearrange("p (j n) -> p j n", j=NJ),
                    attH[:, :, at]).then_inc(s_aL.sem, 1)

            def xp_out(b, m):
                if m == 3:
                    wait(dve, s_p, b, 0)
                elif b > 0:
                    wait(dve, s_p, b - 1, 3 if m == 0 else m)
                src, to = pview(prod[m % 2], b), xb[:, m % 3, :]
                if b == 0:
                    tt(to[:, 16:16 + 272], src[:, 0, :], rms[:, 0:272], ALU.mult)
                    tt(to[:, 16 + 272:XW], src[:, 1, 0:240], rms[:, 272:TB], ALU.mult)
                    ins = tt(to[:, XWMAX - DEC:XWMAX], src[:, 1, 240:272], rms[:, TB:CMAX], ALU.mult)
                else:
                    ins = tt(to[:, 16:XW], src[:, 0, :], rms[:, 0:TB], ALU.mult)
                ins.then_inc(s_xb.sem, 1)

            def scale_gate(b, kind, m, to):
                tt(sview(to, b), pview(prod[m % 2 if kind == "gp" else 0], b), sview(rms, b),
                   ALU.mult).then_inc(s_gz.sem, 1)

            def gate_pool(b, m):
                wait(dve, s_pp, b, m)
                wait(dve, s_gp, b, m)
                h = sview(hT[:, m, :], b)
                stt(out=h, in0=h, scalar=1.0, in1=pview(auxB, b), op0=ALU.add, op1=ALU.mult).then_inc(s_pool.sem, 1)

            def merge(b, i, m):
                n = cols(b)
                wait(dve, s_ga, b, m)
                t = work[:, m % 2, :]
                stt(out=sview(t, b), in0=sview(t, b), scalar=1.0, in1=pview(prod[i % 2], b),
                    op0=ALU.add, op1=ALU.mult).then_inc(s_gat.sem, 1)
                wait(dve, s_gat, b, m)
                wait(dve, s_pool, b, m)
                stt(out=hT[:, m, 0:n], in0=hT[:, m, 0:n], scalar=p_scale[:, m:m + 1], in1=t[:, 0:n],
                    op0=ALU.mult, op1=ALU.add).then_inc(s_mrg.sem, 1)

            def step(b, i):
                kind, m = MIXER[i]
                n = cols(b)
                if kind == "ao":
                    gate_pool(b, m)
                wait_product(dve, b, i)
                if i == NJ + 1:
                    v = work[:, m % 2, :]
                    tt(sview(v, b), pview(prod[i % 2], b), sview(rms, b), ALU.mult).then_inc(s_vn.sem, 1)
                if kind == "xp":
                    xp_out(b, m)
                if kind == "gp":
                    if b > 0:
                        dve.wait_ge(y_out[m // 2], 16 * b)
                    scale_gate(b, kind, m, hT[:, m, :])
                if kind == "ga":
                    scale_gate(b, kind, m, work[:, m % 2, :])
                if kind == "ao":
                    merge(b, i, m)
                if kind == "out":
                    tt(sview(hT[:, m, :], b), sview(xT[:, m, :], b), pview(prod[i % 2], b), ALU.add).then_inc(s_h.sem, 1)
                if b > 0 and i == 0:
                    link(nc.vector.tensor_copy(k_before, k_halves[:, 1, TB // 2 - CH:TB // 2]))
                if i == 6:
                    wait(dve, s_vA, b)
                    if b > 0:
                        link(nc.vector.tensor_copy(vB[CH:P, 0, :], vB[CH:P, NT, :]))
                    nc.vector.tensor_copy(vB[0:CH, 0:NT, :], vA[0:CH, :, :])
                    nc.vector.tensor_copy(vB[CH:P, 1:NT + 1, :], vA[CH:P, :, :]).then_inc(s_vB.sem, 1)
                if 0 <= i - ATT0 - 2 < nchunks(b):
                    attn_low(b, i - ATT0 - 2)
                if 0 <= i - ATT0 < nchunks(b):
                    row_max(b, i - ATT0)
                split_low(b, i + 2)
                if kind == "out":
                    gained_low("h", b, m)
                    add_square("h", b, m)
                if kind == "ao":
                    wait(dve, s_mH, b, m)
                    stt(out=midL[:, m, 0:n], in0=hT[:, m, 0:n], scalar=0.5, in1=f(midH[:, m, 0:n]),
                        op0=ALU.mult, op1=ALU.subtract).then_inc(s_mL.sem, 1)
                if i == 0:
                    invert("x", 0) if b == 0 else invert("f", b - 1)
                if (b, i) == (0, 1):
                    scale_angles(0)
                if 1 <= i <= 5:
                    rotate(b, i - 1)
                if 0 <= i - ATT0 < nchunks(b):
                    norm_probs(b, i - ATT0)

            def up(b, q):
                first = isinstance(q, int) and q == 0
                n = cols(b)
                for m in range(KD):
                    wait_mlp(dve, b, q, m)
                    if first and m == 0:
                        split_low_mlp(b, q, m + 2)
                        wait(dve, s_r, "h", b)
                    stt(out=sview(work[:, m % 2, :], b), in0=pview(prod[m % 2], b), scalar=0.0, in1=sview(rms, b),
                        op0=ALU.max, op1=ALU.mult).then_inc(relu_done, 1)
                    dve.wait_ge(relu_done, hid(b, q, m))
                    if m > 0 or not (first and b == 0):
                        dve.wait_ge(hid_low, hid(b, q, m - 1))
                    tt(work[:, 2, 0:n], work[:, m % 2, 0:n], work[:, m % 2, 0:n], ALU.mult).then_inc(hid_sq, 1)
                    if not (first and m == 0):
                        split_low_mlp(b, q, m + 2)
                    dve.wait_ge(hid_high, hid(b, q, m))
                    dve.wait_ge(hid_sq, hid(b, q, m))
                    low(midL[:, m, 0:n], work[:, 2, 0:n], midH[:, m, 0:n]).then_inc(hid_low, 1)
                    if first and b + 1 < NB and m >= 4:
                        add_square("x", b + 1, 2 * m - 8)
                        add_square("x", b + 1, 2 * m - 7)

            def add_down(b, q, m):
                wait_mlp(dve, b, q, KD + m)
                tt(sview(hT[:, m, :], b), sview(hT[:, m, :], b), pview(prod[m % 2], b), ALU.add).then_inc(down_added, 1)

            def down(b, q):
                for m in range(KD):
                    add_down(b, q, m)
                    split_low_mlp(b, q, KD + m + 2)

            def last_down(b):
                for m in range(KD):
                    add_down(b, NQ - 1, m)
                    split_low(b, UNITS - KD + m + 2)
                    if b + 1 < NB:
                        gained_low("x", b + 1, m)
                        if m == 0:
                            invert("x", b + 1)
                        if m == 3:
                            scale_angles(b + 1)
                    if m >= 2:
                        add_square("f", b, m - 1)
                    if m == KD - 1:
                        add_square("f", b, m)

            split_low(0, 0)
            for k in range(KD):
                gained_low("x", 0, k)
            split_low(0, 1)
            for k in range(KD):
                add_square("x", 0, k)
            nc.vector.tensor_scalar(nsink[:, :], vec[:, 4 * KD:4 * KD + 6], -1.0, None, ALU.mult)
            for b in blocks:
                for i in range(M_MLP):
                    step(b, i)
                invert("h", b)
                quarters(dve, b, up, down, last_down)
            invert("f", NB - 1)
            wait(dve, s_r, "f", NB - 1)
            for k in range(KD):
                final(NB - 1, k)

        @block.gpsimd
        def _(pool):
            tt = nc.gpsimd.tensor_tensor

            def link(ins):
                chain[0] += 1
                ins.then_inc(pool_chain, 1)
                pool.wait_ge(pool_chain, chain[0])

            chain = [0]
            link(nc.gpsimd.memset(ones[:, :], 1.0))
            link(nc.gpsimd.memset(eps, EPS))
            link(nc.gpsimd.memset(k_before, 0.0))
            nc.gpsimd.memset(vB[CH:P, 0, :], 0.0).then_inc(start, 1)
            pool.wait_ge(start, 1)
            pool.wait_ge(const_in, 16)
            pool.wait_ge(sample_in, 48)
            for b in blocks:
                w = XWMAX if b == 0 else XW
                if b > 0:
                    wait(pool, s_r, "f", b - 1)
                    for k in range(KD):
                        n = cols(b - 1)
                        wait(pool, s_fg, b - 1, k)
                        tt(hT[:, k, 0:n], hT[:, k, 0:n], acc[:, 0:n], ALU.mult).then_inc(s_y.sem, 1)
                for g in range(G):
                    x = xb[:, g % 3, :]
                    wait(pool, s_xb, b, g)
                    if b > 0:
                        wait(pool, s_carry, b - 1, g)
                    link(nc.gpsimd.tensor_copy(x[:, 0:16], carry[:, g, :]) if b > 0 else nc.gpsimd.memset(x[:, 0:16], 0.0))
                    if b == 0:
                        link(nc.gpsimd.tensor_copy(x[:, XW:XW + 16], state[:, g, :]))
                        link(nc.gpsimd.tensor_copy(carry_s[:, g, :], x[:, XWMAX - 16:XWMAX]))
                    nc.gpsimd.tensor_copy(carry[:, g, :], x[:, XW - 16:XW]).then_inc(s_carry.sem, 1)
                    src = x
                    for s in range(g + 1):
                        lo, dst = 2 ** (s + 1) - 1, sq[:, s % 2, :]
                        link(tt(dst[:, lo:w], src[:, lo:w], src[:, lo - 2 ** s:w - 2 ** s], ALU.add))
                        src = dst
                    link(nc.gpsimd.tensor_scalar(diff[:, 16:w], src[:, 16:w], 1.0 / 2 ** (g + 1), None, ALU.mult))
                    if b == 0:
                        link(tt(diff[:, 16:32], src[:, 16:32], head_scale[:, g, :], ALU.mult))
                    tt(diff[:, 16:w], diff[:, 16:w], x[:, 16:w], ALU.subtract).then_inc(s_p.sem, 1)
                    wait(pool, s_pH, b, g)
                    ins = tt(midL[:, POOLED + g, 0:TB], diff[:, 16:XW], f(midH[:, POOLED + g, 0:TB]), ALU.subtract)
                    if b == 0:
                        ins = tt(midL[:, POOLED + g, TB:CMAX], diff[:, XWMAX - DEC:XWMAX], f(midH[:, POOLED + g, TB:CMAX]), ALU.subtract)
                    ins.then_inc(s_pL.sem, 1)


def constants():
    eye = np.eye(P, dtype=np.float32)
    head = np.stack([1.0 / np.minimum(np.arange(16) + 1, 2 ** (g + 1)) for g in range(G)]).astype(np.float32)
    consts = np.concatenate([eye, np.tile(head.reshape(1, -1), (P, 1))], axis=1)
    half = ROT // 2
    inv = (np.float32(500000.0) ** (-np.arange(0, 2 * half, 2, dtype=np.float32) / np.float32(2 * half))).astype(np.float32)
    pos = np.concatenate([np.arange(SEQ), PAST + np.arange(DEC)]).astype(np.float32)
    angle = (pos[None, :] * inv[:, None]).astype(np.float32).astype(np.float64)
    tables = np.zeros((P, 2, SEQ + DEC), np.float32)
    tables[:, 0, :] = 1.0
    for at in range(0, P, half):
        if at % HD < 2 * half:
            tables[at:at + half, 0, :] = np.cos(angle)
            tables[at:at + half, 1, :] = np.sin(angle) * (-1 if at % HD == 0 else 1)
    return consts, tables


def unit_layout(w_in, w_pool, w_attn_up, w_out, w_up, w_down):
    def tile(w, cols):
        rows = w.shape[0] // P
        return w[:, cols].reshape(rows, P, P).transpose(1, 0, 2).reshape(P, rows * P)

    def cols(at):
        return np.arange(at, at + P)

    q0, k0 = G * P, G * P + NJ * KV * HD
    gp0 = k0 + 2 * P
    ga0 = gp0 + D
    pooled = w_pool.transpose(1, 0, 2).reshape(P, 2 * G * P)
    up_rows = w_attn_up.reshape(KV, NJ, HD, D).transpose(1, 0, 2, 3).reshape(NJ * P, D)
    q_cols = lambda j: np.concatenate([np.arange(q0 + (g * NJ + j) * HD, q0 + (g * NJ + j + 1) * HD) for g in range(KV)])
    make = {
        "qkv": lambda m: tile(w_in, q_cols(m) if m < NJ else cols(k0 + (m - NJ) * P)),
        "xp": lambda m: tile(w_in, cols(m * P)),
        "gp": lambda m: tile(w_in, cols(gp0 + m * P)),
        "ga": lambda m: tile(w_in, cols(ga0 + m * P)),
        "ao": lambda m: tile(up_rows, cols(m * P)),
        "pool": lambda m: pooled[:, m * P:(m + 1) * P],
        "out": lambda m: tile(w_out, cols(m * P)),
    }
    units = []
    for kind, m in MIXER:
        parts = [make[kind](m)] + ([make["pool"](m)] if kind == "ao" else [])
        units.append(np.concatenate(parts + [np.zeros((P, WIDTH - sum(p.shape[1] for p in parts)), np.float32)], axis=1))
    for q in range(NQ):
        units += [tile(w_up, cols(q * D + m * P)) for m in range(KD)]
        units += [tile(w_down[q * D:(q + 1) * D], cols(m * P)) for m in range(KD)]
    return np.ascontiguousarray(np.stack(units))


def feature_major(x):
    return np.ascontiguousarray(x.T.reshape(KD, P, -1).transpose(1, 0, 2))


def token_major(y):
    return y.transpose(1, 0, 2).reshape(D, -1).T


def kernel(x_prompt, x_sample, cache_k, cache_v, state_pool, norm_mix, w_in, sinks, w_pool, pool_scale,
           w_attn_up, w_out, norm_mlp, w_up, w_down, norm_final):
    import concourse.bacc as bacc
    from concourse.bass_utils import run_bass_kernel_spmd

    xp, xs = np.asarray(x_prompt)[0], np.asarray(x_sample)[0]
    consts, tables = constants()
    by_tile = lambda v: np.asarray(v).reshape(KD, P).T
    s = np.asarray(sinks)[0].reshape(KV, NJ)
    rows = np.arange(P)
    sink_cols = [s[g, 2 * pair + rows // CH] for g in range(KV) for pair in range(2)]
    sink_cols += [s[g, rows // DEC] for g in range(KV)]
    vectors = np.concatenate([by_tile(norm_mix[0]), by_tile(pool_scale[0]), by_tile(norm_mlp[0]), by_tile(norm_final),
                              np.stack(sink_cols, axis=1)], axis=1)
    ck, cv = (np.asarray(c)[0, 0].reshape(CACHE, P) for c in (cache_k, cache_v))
    hist = np.asarray(state_pool)[0, 0].T.reshape(G, P, PBUF).transpose(1, 0, 2)
    arrays = {
        "x0": feature_major(np.concatenate([xp[:TB], xs])),
        "x123": np.stack([feature_major(xp[b * TB:(b + 1) * TB]) for b in range(1, NB)]),
        "weights": unit_layout(*(np.asarray(w)[0] for w in (w_in, w_pool, w_attn_up, w_out, w_up, w_down))),
        "consts": consts, "vectors": vectors, "tables": tables,
        "state_s": np.concatenate([np.zeros((P, G, 1), np.float32), hist], axis=2),
        "kcache_t": ck[CACHE - CH:].T, "vcache": cv[CACHE - CH:],
        "kold": ck[DEC:], "vold": cv[DEC:],
    }
    arrays = {n: np.ascontiguousarray(a) for n, a in arrays.items()}
    outs = {"y0": (P, KD, CMAX), "y123": (NB - 1, P, KD, TB), "k_new": (P, P), "v_new": (P, P), "p_new": (P, G, 16),
            "k_old_out": (CACHE - DEC, P), "v_old_out": (CACHE - DEC, P), "ks_new": (P, DEC), "vs_new": (DEC, P),
            "ps_new": (P, G, 16)}
    nc = bacc.Bacc("TRN2", target_bir_lowering=False, num_devices=1)
    args = [nc.dram_tensor(n, a.shape, F32, kind="ExternalInput").ap() for n, a in arrays.items()]
    args += [nc.dram_tensor(n, shape, F32, kind="ExternalOutput").ap() for n, shape in outs.items()]
    build(nc, *args)
    got = run_bass_kernel_spmd(nc, [arrays], core_ids=[0]).results[0]

    first = token_major(got["y0"])
    rest = [token_major(got["y123"][b]) for b in range(NB - 1)]
    heads = lambda a: np.ascontiguousarray(a).reshape(1, 1, CACHE, KV, HD)
    tail = lambda a: np.ascontiguousarray(a[:, :, 1:].transpose(2, 1, 0)).reshape(1, 1, PBUF, G * P)
    return (np.concatenate([first[:TB], *rest])[None], first[TB:][None],
            heads(got["k_new"].T), heads(got["v_new"]), tail(got["p_new"]),
            heads(np.concatenate([got["k_old_out"], got["ks_new"].T])),
            heads(np.concatenate([got["v_old_out"], got["vs_new"]])),
            tail(got["ps_new"]))
```
